# Optimizing a Trainium2 kernel written in Bass

```python
import math
import jax, jax.numpy as jnp
from jax import lax
import numpy as np

D_MODEL = 1024
BATCH = 1
SEQ = 512
DEPTH = 2

N_A_LAYERS = DEPTH // 2
N_B_LAYERS = DEPTH - N_A_LAYERS

A_HEADS = 16
A_HEAD_DIM = D_MODEL // A_HEADS
A_QKV_WIDTH = 3 * A_HEADS * A_HEAD_DIM
Q_BLOCK = 128

B_GROUPS = ((128, 1), (512, 4), (2048, 16))
B_N_GROUPS = len(B_GROUPS)
B_HEADS_PER_GROUP = 8
B_HEAD_DIM = 64
B_WINDOW_STEPS = 128
B_Q_WIDTH = B_N_GROUPS * B_HEADS_PER_GROUP * B_HEAD_DIM
B_OUT_WIDTH = B_HEADS_PER_GROUP * B_HEAD_DIM
B_KV_WIDTH = 2 * B_Q_WIDTH
ALIBI_TOTAL_HEADS = B_N_GROUPS * B_HEADS_PER_GROUP

D_FF = 2816
CONV_WIDTH = 3

RMS_EPS = 1e-6


def rms_norm(x, g):
    xf = x.astype(jnp.float32)
    y = xf * lax.rsqrt(jnp.mean(xf * xf, axis=-1, keepdims=True) + RMS_EPS)
    return (y * g.astype(jnp.float32)).astype(x.dtype)

def conv_ffn(h, w_up, conv_w, conv_b, w_down):
    u = h @ w_up
    c = u.shape[-1]
    u = lax.conv_general_dilated(
        u, conv_w[:, None, :].astype(u.dtype), window_strides=(1,),
        padding=[(CONV_WIDTH - 1, 0)],
        dimension_numbers=("NWC", "WIO", "NWC"),
        feature_group_count=c) + conv_b
    a, gate = jnp.split(u, 2, axis=-1)
    return (jax.nn.silu(gate) * a) @ w_down

def forgetting_attention(q, k, v, log_f):
    S = q.shape[1]
    dh = q.shape[-1]
    scale = dh ** -0.5
    c = jnp.cumsum(log_f.astype(jnp.float32), axis=1).transpose(0, 2, 1)
    outs = []
    for i in range(S // Q_BLOCK):
        q0 = i * Q_BLOCK
        q1 = q0 + Q_BLOCK
        s = jnp.einsum("bqhd,bkhd->bhqk", q[:, q0:q1], k[:, :q1]).astype(jnp.float32) * scale
        s = s + c[:, :, q0:q1, None] - c[:, :, None, :q1]
        causal = jnp.arange(q0, q1)[:, None] >= jnp.arange(q1)[None, :]
        p = jax.nn.softmax(jnp.where(causal, s, -jnp.inf), axis=-1)
        outs.append(jnp.einsum("bhqk,bkhd->bqhd", p.astype(v.dtype), v[:, :q1]))
    return jnp.concatenate(outs, axis=1)

def dilated_branch(q, k, v, dil, slopes):
    B, S, H, Dh = q.shape
    W = B_WINDOW_STEPS
    period = dil * W
    Sp = -(-S // period) * period
    nb = Sp // period
    pad = ((0, 0), (0, Sp - S), (0, 0), (0, 0))

    def blocks(t):
        return jnp.pad(t, pad).reshape(B, nb, W, dil, H, Dh)

    def with_prev(t):
        prev = jnp.pad(t, ((0, 0), (1, 0), (0, 0), (0, 0), (0, 0), (0, 0)))[:, :nb]
        return jnp.concatenate([prev, t], axis=2)

    qb = blocks(q)
    kk = with_prev(blocks(k))
    vv = with_prev(blocks(v))
    s = jnp.einsum("bnirhd,bnjrhd->bnrhij", qb, kk).astype(jnp.float32) * (Dh ** -0.5)
    qi = jnp.arange(W)[:, None]
    kj = jnp.arange(2 * W)[None, :]
    dist = qi + W - kj
    band = (dist >= 0) & (dist <= W)
    first = (jnp.arange(nb)[:, None, None] == 0) & (kj < W)[None]
    valid = band[None] & ~first
    bias = -slopes[:, None, None] * (dil * dist).astype(jnp.float32)
    s = jnp.where(valid[None, :, None, None], s + bias, -jnp.inf)
    m = jnp.max(s, axis=-1, keepdims=True)
    p = jnp.exp(s - m)
    l = jnp.sum(p, axis=-1, keepdims=True)
    o = jnp.einsum("bnrhij,bnjrhd->bnirhd", (p / l).astype(v.dtype), vv)
    lse = (m + jnp.log(l))[..., 0]
    o = o.reshape(B, Sp, H, Dh)[:, :S]
    lse = lse.transpose(0, 1, 4, 2, 3).reshape(B, Sp, H)[:, :S]
    return o, lse

def first_inputs(seed: int = 0) -> dict:
    key = jax.random.key(seed)
    ks = jax.random.split(key, 16)
    f32 = jnp.float32

    def nrm(k, shape, fan_in):
        return jax.random.normal(k, shape, f32) * (fan_in ** -0.5)

    def gain(k, shape):
        return 1.0 + 0.05 * jax.random.normal(k, shape, f32)

    return {
        "x": jax.random.normal(ks[0], (BATCH, SEQ, D_MODEL), f32),
        "a_w_in": nrm(ks[1], (N_A_LAYERS, D_MODEL, A_QKV_WIDTH + A_HEADS), D_MODEL),
        "a_b_f": 2.0 + 0.1 * jax.random.normal(ks[2], (N_A_LAYERS, A_HEADS), f32),
        "a_w_out": nrm(ks[3], (N_A_LAYERS, A_HEADS * A_HEAD_DIM, D_MODEL), A_HEADS * A_HEAD_DIM),
        "b_w_q": nrm(ks[4], (N_B_LAYERS, D_MODEL, B_Q_WIDTH), D_MODEL),
        "b_w_out": nrm(ks[5], (N_B_LAYERS, B_OUT_WIDTH, D_MODEL), B_OUT_WIDTH),
        "kv_norm_g": gain(ks[6], (D_MODEL,)),
        "w_kv": nrm(ks[7], (D_MODEL, B_KV_WIDTH), D_MODEL),
        "mix_norm_g": gain(ks[8], (DEPTH, D_MODEL)),
        "ffn_norm_g": gain(ks[9], (DEPTH, D_MODEL)),
        "ffn_w_up": nrm(ks[10], (DEPTH, D_MODEL, 2 * D_FF), D_MODEL),
        "ffn_conv_w": nrm(ks[11], (DEPTH, CONV_WIDTH, 2 * D_FF), CONV_WIDTH),
        "ffn_conv_b": 0.02 * jax.random.normal(ks[12], (DEPTH, 2 * D_FF), f32),
        "ffn_w_down": nrm(ks[13], (DEPTH, D_FF, D_MODEL), D_FF),
        "final_norm_g": gain(ks[14], (D_MODEL,)),
    }

def first_block(x, a_w_in, a_b_f, a_w_out, b_w_q, b_w_out, kv_norm_g, w_kv,
              mix_norm_g, ffn_norm_g, ffn_w_up, ffn_conv_w, ffn_conv_b, ffn_w_down,
              final_norm_g):
    B, S, D = x.shape
    slopes = jnp.exp2(-8.0 * jnp.arange(1, ALIBI_TOTAL_HEADS + 1, dtype=jnp.float32)
                      / ALIBI_TOTAL_HEADS).reshape(B_N_GROUPS, B_HEADS_PER_GROUP)
    kv = None
    for layer in range(DEPTH):
        if layer < N_A_LAYERS:
            h = rms_norm(x, mix_norm_g[layer])
            proj = h @ a_w_in[layer]
            qkv = proj[..., :A_QKV_WIDTH].reshape(B, S, 3, A_HEADS, A_HEAD_DIM)
            log_f = jax.nn.log_sigmoid(
                proj[..., A_QKV_WIDTH:].astype(jnp.float32) + a_b_f[layer].astype(jnp.float32))
            o = forgetting_attention(qkv[:, :, 0], qkv[:, :, 1], qkv[:, :, 2], log_f)
            x = x + o.reshape(B, S, A_HEADS * A_HEAD_DIM) @ a_w_out[layer]
        else:
            if kv is None:
                kv = (rms_norm(x, kv_norm_g) @ w_kv).reshape(
                    B, S, 2, B_N_GROUPS, B_HEADS_PER_GROUP, B_HEAD_DIM)
            bl = layer - N_A_LAYERS
            h = rms_norm(x, mix_norm_g[layer])
            q = (h @ b_w_q[bl]).reshape(B, S, B_N_GROUPS, B_HEADS_PER_GROUP, B_HEAD_DIM)
            outs, lses = [], []
            for g, (window, dil) in enumerate(B_GROUPS):
                o_g, lse_g = dilated_branch(q[:, :, g], kv[:, :, 0, g], kv[:, :, 1, g],
                                            dil, slopes[g])
                outs.append(o_g)
                lses.append(lse_g)
            alpha = jax.nn.softmax(jnp.stack(lses, axis=0), axis=0)
            o = jnp.sum(alpha[..., None].astype(outs[0].dtype) * jnp.stack(outs, axis=0), axis=0)
            x = x + o.reshape(B, S, B_OUT_WIDTH) @ b_w_out[bl]
        h = rms_norm(x, ffn_norm_g[layer])
        x = x + conv_ffn(h, ffn_w_up[layer], ffn_conv_w[layer], ffn_conv_b[layer],
                         ffn_w_down[layer])
    return rms_norm(x, final_norm_g)


CHUNK = 64
N_EVEN = (DEPTH + 1) // 2
N_ODD = DEPTH // 2
EPS = 1e-6
ROPE_THETA = 10000.0

GM_GROUPS = 4
GM_GROUP_DIM = 128
GM_WIDTH = GM_GROUPS * GM_GROUP_DIM
GM_BLOCK = 128
MLA_HEADS = 8
MLA_Q_RANK = 384
MLA_KV_RANK = 256
MLA_NOPE = 64
MLA_ROPE = 32
MLA_V = 64
MLA_QK = MLA_NOPE + MLA_ROPE
ATTN_BLOCK = 128
EVEN_IN = 2 * GM_WIDTH + MLA_Q_RANK + MLA_KV_RANK + MLA_ROPE
EVEN_MIX = GM_WIDTH + MLA_HEADS * MLA_V
RET_HEADS = 4
RET_QK = 256
RET_V = 512
ODD_IN = 2 * RET_HEADS * RET_QK + 2 * RET_HEADS * RET_V
ODD_MIX = RET_HEADS * RET_V
D_FF_2 = -(-8 * D_MODEL // (3 * 256)) * 256


def rmsnorm(x, g):
    xf = x.astype(jnp.float32)
    y = xf * lax.rsqrt(jnp.mean(xf * xf, axis=-1, keepdims=True) + EPS)
    return (y * g.astype(jnp.float32)).astype(x.dtype)

def rope(x, pos):
    half = x.shape[-1] // 2
    inv = ROPE_THETA ** (-jnp.arange(half, dtype=jnp.float32) / half)
    ang = pos.astype(jnp.float32)[:, None] * inv[None, :]
    cos = jnp.cos(ang)[None, :, None, :]
    sin = jnp.sin(ang)[None, :, None, :]
    xf = x.astype(jnp.float32)
    x1, x2 = xf[..., :half], xf[..., half:]
    return jnp.concatenate([x1 * cos - x2 * sin, x2 * cos + x1 * sin], axis=-1).astype(x.dtype)

def spatial_gating(u, v, v_norm, w_s, b_s):
    B, S, _ = u.shape
    n = S // GM_BLOCK
    v = rmsnorm(v.reshape(B, S, GM_GROUPS, GM_GROUP_DIM), v_norm)
    cid = jnp.arange(GM_BLOCK) // CHUNK
    w = jnp.where((cid[None, :] <= cid[:, None])[None], w_s, 0)
    vb = v.reshape(B, n, GM_BLOCK, GM_GROUPS, GM_GROUP_DIM)
    s = jnp.einsum('gts,bnsgc->bntgc', w, vb) + b_s.T[:, :, None]
    ub = u.reshape(B, n, GM_BLOCK, GM_GROUPS, GM_GROUP_DIM)
    return (ub * s).reshape(B, S, GM_WIDTH)

def block_causal_attention(q, k, v):
    S = q.shape[1]
    scale = MLA_QK ** -0.5
    chunk_id = jnp.arange(S) // CHUNK
    outs = []
    for start in range(0, S, ATTN_BLOCK):
        end = start + ATTN_BLOCK
        s = jnp.einsum('bqhd,bkhd->bhqk', q[:, start:end], k[:, :end]).astype(jnp.float32) * scale
        mask = chunk_id[None, :end] <= chunk_id[start:end, None]
        p = jax.nn.softmax(jnp.where(mask, s, -jnp.inf), axis=-1).astype(v.dtype)
        outs.append(jnp.einsum('bhqk,bkhd->bqhd', p, v[:, :end]))
    return jnp.concatenate(outs, axis=1)

def mla(c_q, c_kv, k_pe, q_a_norm, w_uq, kv_a_norm, w_ukv, q_norm, k_norm, pos):
    B, S, _ = c_q.shape
    q = (rmsnorm(c_q, q_a_norm) @ w_uq).reshape(B, S, MLA_HEADS, MLA_QK)
    kv = (rmsnorm(c_kv, kv_a_norm) @ w_ukv).reshape(B, S, MLA_HEADS, MLA_NOPE + MLA_V)
    k = jnp.concatenate([kv[..., :MLA_NOPE],
                         jnp.broadcast_to(k_pe[:, :, None, :], (B, S, MLA_HEADS, MLA_ROPE))], axis=-1)
    v = kv[..., MLA_NOPE:]
    q = rmsnorm(q, q_norm)
    k = rmsnorm(k, k_norm)
    q = jnp.concatenate([q[..., :MLA_NOPE], rope(q[..., MLA_NOPE:], pos)], axis=-1)
    k = jnp.concatenate([k[..., :MLA_NOPE], rope(k[..., MLA_NOPE:], pos)], axis=-1)
    o = block_causal_attention(q, k, v)
    return o.reshape(B, S, MLA_HEADS * MLA_V)

def even_mixer(h, w_in, gm_v_norm, gm_w_s, gm_b_s, q_a_norm, w_uq, kv_a_norm, w_ukv,
               q_norm, k_norm, w_out, pos):
    z = h @ w_in
    o1 = GM_WIDTH
    o2 = 2 * GM_WIDTH
    o3 = o2 + MLA_Q_RANK
    o4 = o3 + MLA_KV_RANK
    u = jax.nn.gelu(z[..., :o1])
    v = jax.nn.gelu(z[..., o1:o2])
    a = spatial_gating(u, v, gm_v_norm, gm_w_s, gm_b_s)
    b = mla(z[..., o2:o3], z[..., o3:o4], z[..., o4:], q_a_norm, w_uq, kv_a_norm, w_ukv,
            q_norm, k_norm, pos)
    return jnp.concatenate([a, b], axis=-1) @ w_out

def retention(q, k, v):
    B, S, H, dk = q.shape
    dv = v.shape[-1]
    n = S // CHUNK
    lg = jnp.log(1.0 - 2.0 ** (-5.0 - jnp.arange(H, dtype=jnp.float32)))
    j = jnp.arange(CHUNK, dtype=jnp.float32)
    diff = j[:, None] - j[None, :]
    dmask = jnp.where(diff >= 0, jnp.exp(lg[:, None, None] * jnp.maximum(diff, 0.0)), 0.0)
    xi = jnp.exp(lg[:, None] * (j + 1.0))[None, :, :, None]
    zeta = jnp.exp(lg[:, None] * (CHUNK - 1.0 - j))[None, :, :, None]
    g_chunk = jnp.exp(lg * CHUNK)[None, :, None, None]

    def to_chunks(t):
        return t.astype(jnp.float32).reshape(B, n, CHUNK, H, -1).transpose(1, 0, 3, 2, 4)

    qc = to_chunks(q)
    kc = to_chunks(k) * (dk ** -0.5)
    vc = to_chunks(v)

    def step(state, inp):
        qi, ki, vi = inp
        a = jnp.einsum('bhjd,bhmd->bhjm', qi, ki) * dmask
        o = jnp.einsum('bhjm,bhme->bhje', a, vi) + jnp.einsum('bhjd,bhde->bhje', qi, state) * xi
        state = state * g_chunk + jnp.einsum('bhmd,bhme->bhde', ki * zeta, vi)
        return state, o

    state0 = jnp.zeros((B, H, dk, dv), jnp.float32)
    _, o = lax.scan(step, state0, (qc, kc, vc))
    return o.transpose(1, 0, 3, 2, 4).reshape(B, S, H, dv)

def odd_mixer(h, w_in, out_norm, w_out, pos):
    B, S, _ = h.shape
    nq = RET_HEADS * RET_QK
    nv = RET_HEADS * RET_V
    z = h @ w_in
    q = rope(z[..., :nq].reshape(B, S, RET_HEADS, RET_QK), pos)
    k = rope(z[..., nq:2 * nq].reshape(B, S, RET_HEADS, RET_QK), pos)
    v = z[..., 2 * nq:2 * nq + nv].reshape(B, S, RET_HEADS, RET_V)
    g = z[..., 2 * nq + nv:]
    o = rmsnorm(retention(q, k, v), out_norm)
    o = o.reshape(B, S, nv).astype(h.dtype) * jax.nn.silu(g)
    return o @ w_out

def swiglu(h, w_gate, w_up, w_down):
    return (jax.nn.silu(h @ w_gate) * (h @ w_up)) @ w_down

def second_inputs(seed: int = 0) -> dict:
    key = jax.random.key(seed)
    ks = jax.random.split(key, 24)
    f32 = jnp.float32

    def w(k, shape, fan_in):
        return jax.random.normal(k, shape, f32) * (fan_in ** -0.5)

    def gain(k, shape):
        return 1.0 + 0.1 * jax.random.normal(k, shape, f32)

    return {
        "x": jax.random.normal(ks[0], (BATCH, SEQ, D_MODEL), f32),
        "norm_mix": gain(ks[1], (DEPTH, D_MODEL)),
        "norm_ffn": gain(ks[2], (DEPTH, D_MODEL)),
        "even_w_in": w(ks[3], (N_EVEN, D_MODEL, EVEN_IN), D_MODEL),
        "gm_v_norm": gain(ks[4], (N_EVEN, GM_GROUPS, GM_GROUP_DIM)),
        "gm_w_s": w(ks[5], (N_EVEN, GM_GROUPS, GM_BLOCK, GM_BLOCK), GM_BLOCK),
        "gm_b_s": gain(ks[6], (N_EVEN, GM_GROUPS, GM_BLOCK)),
        "mla_q_a_norm": gain(ks[7], (N_EVEN, MLA_Q_RANK)),
        "mla_w_uq": w(ks[8], (N_EVEN, MLA_Q_RANK, MLA_HEADS * MLA_QK), MLA_Q_RANK),
        "mla_kv_a_norm": gain(ks[9], (N_EVEN, MLA_KV_RANK)),
        "mla_w_ukv": w(ks[10], (N_EVEN, MLA_KV_RANK, MLA_HEADS * (MLA_NOPE + MLA_V)), MLA_KV_RANK),
        "mla_q_norm": gain(ks[11], (N_EVEN, MLA_QK)),
        "mla_k_norm": gain(ks[12], (N_EVEN, MLA_QK)),
        "even_w_out": w(ks[13], (N_EVEN, EVEN_MIX, D_MODEL), EVEN_MIX),
        "odd_w_in": w(ks[14], (N_ODD, D_MODEL, ODD_IN), D_MODEL),
        "ret_out_norm": gain(ks[15], (N_ODD, RET_HEADS, RET_V)),
        "odd_w_out": w(ks[16], (N_ODD, ODD_MIX, D_MODEL), ODD_MIX),
        "ffn_w_gate": w(ks[17], (DEPTH, D_MODEL, D_FF_2), D_MODEL),
        "ffn_w_up": w(ks[18], (DEPTH, D_MODEL, D_FF_2), D_MODEL),
        "ffn_w_down": w(ks[19], (DEPTH, D_FF_2, D_MODEL), D_FF_2),
    }

def second_block(x, norm_mix, norm_ffn, even_w_in, gm_v_norm, gm_w_s, gm_b_s,
              mla_q_a_norm, mla_w_uq, mla_kv_a_norm, mla_w_ukv, mla_q_norm, mla_k_norm,
              even_w_out, odd_w_in, ret_out_norm, odd_w_out,
              ffn_w_gate, ffn_w_up, ffn_w_down):
    pos = jnp.arange(x.shape[1])
    for l in range(DEPTH):
        i = l // 2
        h = rmsnorm(x, norm_mix[l])
        if l % 2 == 0:
            mix = even_mixer(h, even_w_in[i], gm_v_norm[i], gm_w_s[i], gm_b_s[i],
                             mla_q_a_norm[i], mla_w_uq[i], mla_kv_a_norm[i], mla_w_ukv[i],
                             mla_q_norm[i], mla_k_norm[i], even_w_out[i], pos)
        else:
            mix = odd_mixer(h, odd_w_in[i], ret_out_norm[i], odd_w_out[i], pos)
        x = x + mix
        h = rmsnorm(x, norm_ffn[l])
        x = x + swiglu(h, ffn_w_gate[l], ffn_w_up[l], ffn_w_down[l])
    return x


def setup_inputs(seed=0):
    out = dict(first_inputs(seed))
    for name, value in second_inputs(seed + 1).items():
        if name != "x":
            out[name + "_2"] = value
    return out


def reference(
    x, a_w_in, a_b_f, a_w_out, b_w_q, b_w_out, kv_norm_g, w_kv, mix_norm_g, ffn_norm_g,
    ffn_w_up, ffn_conv_w, ffn_conv_b, ffn_w_down, final_norm_g, norm_mix_2, norm_ffn_2,
    even_w_in_2, gm_v_norm_2, gm_w_s_2, gm_b_s_2, mla_q_a_norm_2, mla_w_uq_2, mla_kv_a_norm_2,
    mla_w_ukv_2, mla_q_norm_2, mla_k_norm_2, even_w_out_2, odd_w_in_2, ret_out_norm_2,
    odd_w_out_2, ffn_w_gate_2, ffn_w_up_2, ffn_w_down_2,
):
    x = first_block(
        x, a_w_in, a_b_f, a_w_out, b_w_q, b_w_out, kv_norm_g, w_kv, mix_norm_g, ffn_norm_g,
        ffn_w_up, ffn_conv_w, ffn_conv_b, ffn_w_down, final_norm_g,
    )
    return second_block(
        x, norm_mix_2, norm_ffn_2, even_w_in_2, gm_v_norm_2, gm_w_s_2, gm_b_s_2, mla_q_a_norm_2,
        mla_w_uq_2, mla_kv_a_norm_2, mla_w_ukv_2, mla_q_norm_2, mla_k_norm_2, even_w_out_2,
        odd_w_in_2, ret_out_norm_2, odd_w_out_2, ffn_w_gate_2, ffn_w_up_2, ffn_w_down_2,
    )


_drawn_inputs = setup_inputs


def setup_inputs(seed=0):
    import zlib

    import numpy as np

    out = dict(_drawn_inputs(seed))
    spreads = {}
    factors = {'mla_q_a_norm_2': 4.993,
     'mla_kv_a_norm_2': 3.434,
     'mla_q_norm_2': 4.904,
     'mla_k_norm_2': 5.011,
     'gm_v_norm_2': 3.221,
     'gm_b_s_2': 2.843,
     'ret_out_norm_2': 3.09}
    for name, (base, spread) in spreads.items():
        noise = np.random.default_rng([zlib.crc32(name.encode()), seed]).standard_normal(out[name].shape)
        drawn = base * np.exp(spread * noise) if base else spread * noise
        out[name] = __import__('jax').numpy.asarray(drawn.astype(out[name].dtype))
    for name, factor in factors.items():
        out[name] = (out[name] * factor).astype(out[name].dtype)
    return out
```

```python
from contextlib import ExitStack

import numpy as np

import concourse.bass as bass
from concourse import mybir

F32 = mybir.dt.float32
F32R = mybir.dt.float32r
BF16 = mybir.dt.bfloat16
U16 = mybir.dt.uint16
ALU = mybir.AluOpType
ACT = mybir.ActivationFunctionType
AX = mybir.AxisListType.X

S = 512
D = 1024
EPS = 1e-6
NEG = -1.0e38
CT = 8
NRAW = 3
NSP = 4

_COLS = [("mix0", 8), ("ffn0", 8), ("kvn", 8), ("mix1", 8), ("ffn1", 8), ("fin", 8),
         ("m2_0", 8), ("f2_0", 8), ("m2_1", 8), ("f2_1", 8),
         ("cw0", 132), ("cb0", 44), ("cw1", 132), ("cb1", 44),
         ("qa", 3), ("kva", 2), ("gq", 1), ("gk", 1), ("gq1", 1), ("gk1", 1), ("gmv", 4), ("ret", 16), ("bf", 1), ("eps", 1)]
COL = {}
_n = 0
for _name, _k in _COLS:
    COL[_name] = (_n, _k)
    _n += _k
NCOL = _n


def stream_plan():
    out = []

    def fm(name, K, groups, k0=0):
        for g in groups:
            for k in range(K):
                for m in g:
                    out.append((name, k0 + k, m))

    def tm(name, K, cgs, k0=0):
        while len(out) % 4:
            out.append(None)
        for g in cgs:
            for k in range(K):
                for m in g:
                    out.append((name, k0 + k, m))

    def ffn(up, dn):
        for h in range(2):
            fm(up, 8, [[11 * h + j, 22 + 11 * h + j] for j in range(11)])
            fm(dn, 11, DG, 11 * h)

    fm("ain", 8, [[24, 0]] + [[m] for m in range(1, 16)])
    tm("ain", 8, [range(16, 20), range(20, 24)])
    fm("aout", 8, DG)
    ffn("up0", "dn0")
    fm("bq", 8, [[0, 1]] + [[m] for m in range(2, 12)])
    fm("kv", 8, [[0, 1]] + [[m] for m in range(2, 12)])
    tm("kv", 8, [range(12, 16), range(16, 20), range(20, 24)])
    fm("bout", 4, DG)
    ffn("up1", "dn1")
    fm("ei", 8, [[0, 1]] + [[m] for m in range(2, 10)])
    tm("ei", 8, [range(10, 14)])
    fm("uq", 3, [[m] for m in range(8)])
    fm("ukv", 2, [[m] for m in range(8)])
    tm("ukv", 2, [range(8, 12)])
    fm("eout", 8, DG)
    ffn("gu0", "sd0")
    fm("oi", 8, [[0, 1]] + [[m] for m in range(2, 16)])
    tm("oi", 8, [range(16 + 4 * c, 20 + 4 * c) for c in range(4)])
    for h in range(2):
        fm("oi", 8, [[32 + 8 * h + m] for m in range(8)])
        fm("oout", 8, DG, 8 * h)
    ffn("gu1", "sd1")
    while len(out) % CT:
        out.append(None)
    return out


DG = [[0, 1, 2, 3], [4], [5], [6], [7]]


class Eng:

    def __init__(self, name, sem):
        self.name, self.sem, self.q, self.n, self.seen = name, sem, [], 0, {}

    def wait(self, *toks):
        for t in toks:
            if t is None or t[-1:] == (0,):
                continue
            if isinstance(t, list):
                self.wait(*t)
                continue
            s, v = t
            if self.seen.get(id(s), 0) < v:
                self.seen[id(s)] = v
                self.q.append(("w", s, v))

    def do(self, fn, *toks, inc=True):
        self.wait(*toks)
        rec = ["i", fn, None]
        self.q.append(rec)
        if inc:
            return self.mark()
        return None

    def mark(self):
        rec = self.q[-1]
        assert rec[0] == "i"
        if rec[2] is None:
            self.n += 1
            rec[2] = (self.sem, 1)
            self.last = (self.sem, self.n)
        return self.last

    def dma(self, out, in_, sem, *toks):
        self.wait(*toks)
        self.q.append(["i", lambda e: e.dma_start(out, in_), (sem[0], 16)])
        sem[1] += 16
        return (sem[0], sem[1])

    def play(self, e):
        for r in self.q:
            if r[0] == "w":
                e.wait_ge(r[1], r[2])
            else:
                i = r[1](e)
                if r[2]:
                    i.then_inc(*r[2])


class Ring:

    def __init__(self, bufs):
        self.b, self.free, self.i = bufs, [[] for _ in bufs], 0

    def get(self):
        i = self.i % len(self.b)
        self.i += 1
        t, self.free[i] = self.free[i], []
        return i, self.b[i], t


def build(nc, a, stop=99):
    plan = stream_plan()
    ctx = ExitStack()
    with ctx:
        def sb(name, shape, dt=F32, c=None):
            return (c or ctx).enter_context(nc.sbuf_tensor("m_" + name, shape, dt))

        def sem(name):
            return ctx.enter_context(nc.semaphore(name))

        PE, AC, DV, PO = (Eng(n, sem(f"s_{n}")) for n in ("pe", "act", "dve", "pool"))
        SP = Eng("sp", None)
        dsem = {}

        def pool(fn, *toks):
            return PO.do(fn, (PO.sem, PO.n), *toks)

        def dma_sem(name):
            if name not in dsem:
                dsem[name] = [sem(f"d_{name}"), 0]
            return dsem[name]

        ps = [ctx.enter_context(nc.psum_tensor(f"ps{i}", [128, 512], F32)) for i in range(8)]
        bank_free = [[] for _ in range(8)]

        class Banks:
            def __init__(self, ids):
                self.ids, self.i = ids, 0

            def get(self):
                b = self.ids[self.i % len(self.ids)]
                self.i += 1
                t, bank_free[b] = bank_free[b], []
                return b, ps[b], t

        main = Banks([0, 1, 2, 3, 4, 5])
        side = Banks([6, 7])

        x = sb("x", [128, 8, S])
        xs = sb("xs", [128, 8, 2, S], F32R)
        raw = [sb(f"raw{i}", [128, CT * 128]) for i in range(NRAW)]
        wsp = [sb(f"wsp{i}", [128, 2, CT * 128], F32R) for i in range(NSP)]
        cf = sb("cf", [128, NCOL])
        ident = sb("ident", [128, 128])
        identb = sb("identb", [128, 128], BF16)
        maskb = sb("maskb", [128, 2, 128], BF16)
        ones = sb("ones", [128, 128])
        rb2 = [sb(f"rb{i}", [128, S]) for i in range(2)]
        diag = sb("diag", [128, S])
        sqr = Ring([sb(f"sq{i}", [128, S]) for i in range(2)])
        rcol2 = [sb(f"rcol{i}", [128, 8]) for i in range(2)]

        def col(name, i=0, p0=0, p1=128):
            c = COL[name][0] + i
            return cf[p0:p1, c:c + 1]

        t_cf = SP.dma(cf[:, :], a["cf"], dma_sem("cf"))
        t_x = []
        for h in range(4):
            t_x.append(SP.dma(x[:, 2 * h:2 * h + 2, :], a["xT"][:, 2 * h:2 * h + 2, :], dma_sem(f"x{h}")))
        t_id = PO.dma(ident[:, :], a["ident"], dma_sem("id"))
        t_idb = PO.dma(identb[:, :].bitcast(U16), a["identb"], dma_sem("idb"))
        t_mk = PO.dma(maskb[:, :, :].bitcast(U16), a["maskb"], dma_sem("mk"))
        t_ones = DV.do(lambda e: e.memset(ones[:, :], 1.0))

        nch = len(plan) // CT
        raw_tok = {}
        raw_free = {}
        sp_tok = {}
        sp_free = {}
        st = {"load": 0, "split": 0, "i": 0}

        def load_next():
            n = st["load"]
            if n >= nch:
                return
            st["load"] += 1
            raw_tok[n] = SP.dma(raw[n % NRAW][:, :], a["w"][n], dma_sem(f"w{n % NRAW}"), raw_free.get(n - NRAW))

        def split_next():
            n = st["split"]
            if n >= nch:
                return
            st["split"] += 1
            r, w = raw[n % NRAW], wsp[n % NSP]
            t_hi = AC.do(lambda e: e.activation(w[:, 0, :], r[:, :], ACT.Copy), raw_tok[n], sp_free.get(n - NSP))
            t_lo = DV.do(lambda e: e.tensor_tensor(w[:, 1, :], r[:, :], w[:, 0, :].bitcast(F32), ALU.subtract),
                         t_hi, sp_free.get(n - NSP))
            sp_tok[n] = t_lo
            raw_free[n] = [t_hi, t_lo]
            load_next()

        for _ in range(NRAW):
            load_next()

        def use(want, n=1):
            while plan[st["i"]] is None:
                st["i"] += 1
            i = st["i"]
            c = i // CT
            if i % CT == 0 and c > 0:
                sp_free[c - 1] = PE.mark()
            while st["split"] < min(c + NSP, nch):
                split_next()
            assert plan[i] == want, (plan[i], want)
            st["i"] += n
            o = (i % CT) * 128
            w = wsp[c % NSP]
            return w[:, 0, o:o + 128 * n], w[:, 1, o:o + 128 * n], sp_tok[c]

        deferred = []

        def defer(fn, after=3):
            deferred.append([after, fn])

        def tick(k=1):
            for d in deferred:
                d[0] -= k
            while deferred and deferred[0][0] <= 0:
                deferred.pop(0)[1]()

        def flush():
            while deferred:
                deferred.pop(0)[1]()

        def mm3(out, lh, ll, rh, rl, first, last, *toks):
            PE.do(lambda e: e.matmul(out, lh, rh, start=first, stop=False), *toks, inc=False)
            PE.do(lambda e: e.matmul(out, lh, rl, start=False, stop=False), inc=False)
            PE.do(lambda e: e.matmul(out, ll, rh, start=False, stop=last), inc=False)

        def lin_fm(name, K, groups, rhs, evac, k0=0, banks=None):
            for g in groups:
                got = {m: (banks or main).get() for m in g}
                done = {}
                for k in range(K):
                    for m in g:
                        wh, wl, tw = use((name, k0 + k, m))
                        h, l, tr = rhs(k)
                        mm3(got[m][1][:, :], wh, wl, h, l, k == 0, k == K - 1, tw, tr, got[m][2] if k == 0 else None)
                        if k == K - 1:
                            done[m] = PE.mark()
                        tick()
                for m in g:
                    bank_free[got[m][0]] = evac(m, got[m][1], done[m])

        def lin_tm(name, K, cgs, lhs, evac, k0=0, stride=lambda ci: False):
            while st["i"] % 4:
                assert plan[st["i"]] is None
                st["i"] += 1
            for ci, g in enumerate(cgs):
                got = [main.get() for _ in range(4)]
                done = {}
                for k in range(K):
                    wh, wl, tw = use((name, k0 + k, g[0]), 4)
                    h, l, tr = lhs(k)
                    for tb in range(4):
                        o = slice(tb, S, 4) if stride(ci) else slice(tb * 128, tb * 128 + 128)
                        mm3(got[tb][1][:, :], h[:, o], l[:, o], wh, wl, k == 0, k == K - 1,
                            tw, tr, got[tb][2] if k == 0 else None)
                        if k == K - 1:
                            done[tb] = PE.mark()
                    tick(4)
                for tb in range(4):
                    bank_free[got[tb][0]] = evac(ci, tb, got[tb][1], done[tb])

        xs_tok = [None] * 8
        xs_read = [[] for _ in range(8)]
        norm = {"n": 0, "sq": 0, "xread": [None] * 8}

        def stats_cols(n, k, K, sq_ap, tok, st_, free):
            def fn():
                b = st_["bank"] if k else side.get()
                st_["bank"] = b
                for tb in range(4):
                    PE.do(lambda e, tb=tb: e.matmul(b[1][:, tb:tb + 1], sq_ap[:, tb * 128:tb * 128 + 128], ones[:, 0:1],
                                                    start=(k == 0 and tb == 0), stop=(k == K - 1),
                                                    skip_group_check=True),
                          tok, t_ones, b[2] if k == 0 else None, inc=False)
                free.append(PE.mark())
                norm["sq"] -= 1
            return fn

        def finish_stats(st_, dim, n, rb, rc, rb_free, out):
            def fn():
                b = st_["bank"]
                t = AC.do(lambda e: e.activation(rc[:, 4:8], b[1][:, 0:4], ACT.Sqrt, scale=1.0 / dim, bias=col("eps")),
                          PE.mark(), t_cf, rb_free)
                bank_free[b[0]] = [t]
                t = DV.do(lambda e: e.reciprocal(rc[:, 0:4], rc[:, 4:8]), t, rb_free)
                out["col"] = t
                t = DV.do(lambda e: e.tensor_tensor(
                    diag[:, :].rearrange("p (b q) -> p b q", b=4),
                    ident[:, :].rearrange("p (o q) -> p o q", o=1).broadcast_to([128, 4, 128]),
                    rc[:, 0:4].rearrange("p (b o) -> p b o", o=1).broadcast_to([128, 4, 128]), ALU.mult),
                    t, t_id, norm.get("diag"))

                def fn2():
                    c = side.get()
                    PE.do(lambda e: e.matmul(c[1][:, :], ones[:, :], diag[:, :], start=True, stop=True), t, c[2])
                    tp = norm["diag"] = PE.mark()
                    out["row"] = AC.do(lambda e: e.activation(rb[:, :], c[1][:, :], ACT.Copy), tp, rb_free)
                    bank_free[c[0]] = [out["row"]]
                defer(fn2, 3)
            return fn

        cur = {}

        def rms_begin(gain):
            n = norm["n"] = norm["n"] + 1
            r = {"st": {}, "gain": gain, "rb": rb2[n % 2], "rc": rcol2[n % 2], "n": n}
            cur["next"] = r
            return r

        def split_x(k, gain, tx):
            g = col(gain, k)
            t1 = AC.do(lambda e: e.activation(xs[:, k, 0, :], x[:, k, :], ACT.Copy, scale=g), tx, t_cf, xs_read[k])
            t2 = DV.do(lambda e: e.scalar_tensor_tensor(out=xs[:, k, 1, :], in0=x[:, k, :], scalar=g,
                                                        in1=xs[:, k, 0, :].bitcast(F32), op0=ALU.mult,
                                                        op1=ALU.subtract), t1, tx, xs_read[k])
            xs_read[k] = []
            xs_tok[k] = t2

        def sq_room():
            while norm["sq"] >= 2:
                deferred.pop(0)[1]()
            norm["sq"] += 1

        def post_x(r, k, tx):
            if r["gain"] == "":
                return
            if r["gain"] is not None:
                split_x(k, r["gain"], tx)
            sq_room()
            i, sq, free = sqr.get()
            t = AC.do(lambda e: e.activation(sq[:, :], x[:, k, :], ACT.Square), tx, free)
            norm["xread"][k] = t
            defer(stats_cols(0, k, 8, sq, t, r["st"], sqr.free[i]), 3)
            if k == 7:
                defer(finish_stats(r["st"], D, r["n"], r["rb"], r["rc"], r.get("free", []), r), 0)

        def rhs_x(k):
            return xs[:, k, 0, :], xs[:, k, 1, :], xs_tok[k]

        def need_row(r):
            if "row" not in r:
                flush()
            return r["row"]

        x_tok = [t_x[k // 2] for k in range(8)]

        def evac_res(r):
            def evac(m, b, tok):
                t = DV.do(lambda e: e.tensor_tensor(x[:, m, :], x[:, m, :], b[:, :], ALU.add), tok, x_tok[m])
                x_tok[m] = t
                if r is not None:
                    post_x(r, m, t)
                return [t]
            return evac

        def xs_done():
            t = PE.mark()
            for k in range(8):
                xs_read[k] = [t]

        def fence():
            flush()
            toks = [PE.mark()] + [(e.sem, e.n) for e in (AC, DV, PO) if e.n]
            for e in (AC, DV, PO):
                e.wait(*toks)
            return toks

        def split_from(t_in, v, dst, k, free=None):
            t1 = AC.do(lambda e: e.activation(dst[:, k, 0, :], v, ACT.Copy), t_in, free)
            return DV.do(lambda e: e.tensor_tensor(dst[:, k, 1, :], v, dst[:, k, 0, :].bitcast(F32), ALU.subtract),
                         t1, t_in, free)

        def attention(units, oevac, c, pre, bufs=None):
            P = Ring([sb(f"{pre}P{i}", [128, S], F32, c) for i in range(4)])
            PT = Ring([sb(f"{pre}PT{i}", [128, S], F32, c) for i in range(4)])
            stt = Ring([sb(f"{pre}st{i}", [128, 16], F32, c) for i in range(4)])
            sbank = Banks([0, 1, 2, 3])
            tbank = Banks([4, 5])
            obank = Banks([6, 7])
            ob = {}

            def scores(u):
                def one(j):
                    j["toks"] = [t() if callable(t) else t for t in j["toks"]]
                    b, pb, fr = sbank.get()
                    j["sb"] = b
                    for s in j["segs"]:
                        c0, n = s["c0"], s["n"]
                        ex = s.get("extra", [])
                        PE.do(lambda e, c0=c0, n=n, s=s: e.matmul(pb[:, c0:c0 + n], s["q"], s["k"], start=True,
                                                                  stop=not s.get("extra")), fr, j["toks"], inc=False)
                        for ei, (o, m, lt, rh, tk) in enumerate(ex):
                            PE.do(lambda e, o=o, m=m, lt=lt, rh=rh, c0=c0, z=ei == len(ex) - 1: e.matmul(
                                pb[:, c0 + o:c0 + o + m], lt, rh, start=False, stop=z),
                                tk, inc=False)
                    j["ts"] = PE.mark()
                for j in u["jobs"]:
                    one(j)
                if "after_scores" in u:
                    u["after_scores"](PE.mark())

            def soft(u):
                def one(j):
                    b = j["sb"]
                    pb = ps[b]
                    i, P_, fr = P.get()
                    j["pi"], j["P"] = i, P_
                    ii, st_, fr2 = stt.get()
                    ns = len(j["segs"])
                    w = sum(s["n"] for s in j["segs"])
                    tm = None
                    if j["segs"][0].get("bias") is None:
                        for si, s in enumerate(j["segs"]):
                            tm = DV.do(lambda e, si=si, s=s: e.reduce_max(st_[:, si:si + 1],
                                                                          pb[:, s["c0"]:s["c0"] + s["n"]], AX),
                                       j["ts"], fr2)
                    else:
                        for si, s in enumerate(j["segs"]):
                            tm = DV.do(lambda e, si=si, s=s: e.tensor_tensor_reduce(
                                out=P_[:, s["c0"]:s["c0"] + s["n"]], in0=pb[:, s["c0"]:s["c0"] + s["n"]],
                                in1=s["bias"], scale=1.0, scalar=-3.0e38, op0=ALU.add, op1=ALU.max,
                                accum_out=st_[:, si:si + 1]), j["ts"], fr2, fr, s["btok"])
                        bank_free[b] = [tm]
                    tn = DV.do(lambda e: e.tensor_scalar(st_[:, 4:4 + ns], st_[:, 0:ns], -1.0, None, ALU.mult), tm)
                    te = None
                    for si, s in enumerate(j["segs"]):
                        src = pb if s.get("bias") is None else P_
                        te = AC.do(lambda e, si=si, s=s, src=src: e.activation(
                            P_[:, s["c0"]:s["c0"] + s["n"]], src[:, s["c0"]:s["c0"] + s["n"]], ACT.Exp,
                            bias=st_[:, 4 + si:5 + si], accum_out=st_[:, 8 + si:9 + si]), tn, fr)
                    if j["segs"][0].get("bias") is None:
                        bank_free[b] = [te]
                    j["st"], j["te"], j["si"] = st_, te, ii
                    tr = DV.do(lambda e: e.reciprocal(st_[:, 12:12 + ns], st_[:, 8:8 + ns]), te)
                    fin = [tr]
                    if "keep" in j:
                        kl, km = j["keep"]
                        t1 = DV.do(lambda e: e.tensor_copy(kl, st_[:, 8:8 + ns]), te)
                        t2 = DV.do(lambda e: e.tensor_copy(km, st_[:, 0:ns]), te)
                        fin += [t1, t2]
                    for si, s in enumerate(j["segs"]):
                        tp = DV.do(lambda e, si=si, s=s: e.tensor_scalar(
                            P_[:, s["c0"]:s["c0"] + s["n"]], P_[:, s["c0"]:s["c0"] + s["n"]],
                            st_[:, 12 + si:13 + si], None, ALU.mult), tr)
                    stt.free[ii] = fin + [tp]
                    j["tp"] = tp
                    j["w"] = w
                for j in u["jobs"]:
                    one(j)

            def transp(u):
                def one(j):
                    b, pb, fr = tbank.get()
                    P_ = j["P"]
                    for o in range(0, j["w"], 128):
                        PE.do(lambda e, o=o: e.transpose(pb[:, o:o + 128], P_[:, o:o + 128], ident[:, :]),
                              j["tp"], t_id, fr, inc=False)
                    tt = PE.mark()
                    P.free[j["pi"]] = [tt]
                    i, PT_, fr = PT.get()
                    j["PT"], j["pti"] = PT_, i
                    w = j["w"]
                    j["tpt"] = AC.do(lambda e: e.activation(PT_[:, 0:w], pb[:, 0:w], ACT.Copy), tt, fr)
                    bank_free[b] = [j["tpt"]]
                for j in u["jobs"]:
                    one(j)

            def pv(u):
                if u["first"]:
                    ob["b"] = obank.get()
                b, pb, fr = ob["b"]
                lists = []
                for j in u["jobs"]:
                    l = []
                    for s in j["segs"]:
                        nb = len(s["v"])
                        for bi, v in enumerate(s["v"]):
                            l.append((j, s["c0"] + 128 * bi, v, s["oc"], bi == 0, bi == nb - 1))
                    lists.append(l)
                for i in range(max(len(l) for l in lists)):
                    for l in lists:
                        if i < len(l):
                            j, c0, v, oc, f, z = l[i]
                            PE.do(lambda e, j=j, c0=c0, v=v, oc=oc, f=f, z=z: e.matmul(
                                pb[64 * j["par"]:64 * j["par"] + 64, oc:oc + 128], v, j["PT"][:, c0:c0 + 128],
                                start=f, stop=z), j["tpt"], j["vtok"], fr, inc=False)
                t = PE.mark()
                for j in u["jobs"]:
                    PT.free[j["pti"]] = [t]
                if u["last"]:
                    bank_free[b] = oevac(u, pb, t)

            n = len(units)
            for i in range(n + 2):
                if i < n:
                    if "before" in units[i]:
                        units[i]["before"]()
                    scores(units[i])
                    soft(units[i])
                    if "after_soft" in units[i]:
                        units[i]["after_soft"]((DV.sem, DV.n))
                if 1 <= i <= n:
                    transp(units[i - 1])
                if i >= 2:
                    pv(units[i - 2])

        def padded(c, pre, n=2):
            bufs = [[sb(f"{pre}qz{p}{i}", [128, S], F32, c) for i in range(n)] for p in range(2)]
            rings = []
            for p in range(2):
                r = Ring(bufs[p])
                for i, b in enumerate(bufs[p]):
                    t = pool(lambda e, b=b, p=p: e.memset(b[64 * (1 - p):64 * (1 - p) + 64, :], 0.0))
                    r.free[i] = [t]
                rings.append(r)
            return rings

        def pad_q(rings, par, src, tok):
            i, b, fr = rings[par].get()
            t = pool(lambda e: e.tensor_copy(b[64 * par:64 * par + 64, :], src[64 * par:64 * par + 64, :]), tok, fr)
            return i, b, t

        r = rms_begin("mix0")
        for k in range(8):
            post_x(r, k, t_x[k // 2])
        with ExitStack() as c:
            qa = sb("A_q", [128, 8, S], F32, c)
            ka = sb("A_k", [128, 8, S], F32, c)
            va = sb("A_v", [128, 4, 1024], F32, c)
            c3 = sb("A_c3", [128, S], BF16, c)
            sel = sb("A_sel", [128, 16, 128], BF16, c)
            cw = [sb(f"A_cw{i}", [16, S], F32, c) for i in range(4)]
            onr = sb("A_onr", [16, S], F32, c)
            cmid = sb("A_cmid", [16, S], BF16, c)
            qz = padded(c, "A_")
            t_sel = PO.dma(sel[:, :, :].bitcast(U16), a["sel"], dma_sem("sel"))
            t_c3z = pool(lambda e: e.memset(c3[:, :], 0.0))
            t_onr = pool(lambda e: e.memset(onr[:, :], 1.0))
            tq = {}

            def forget(b, tok):
                z, s1, s2, s3 = cw
                rb = r["rb"]
                tr = need_row(r)
                t = DV.do(lambda e: e.tensor_tensor(z[:, :], b[0:16, :], rb[0:16, :], ALU.mult), tok, tr)
                rel = [t]
                t = DV.do(lambda e: e.tensor_scalar(z[:, :], z[:, :], col("bf", 0, 0, 16), None, ALU.add), t, t_cf)
                t1 = AC.do(lambda e: e.activation(s1[:, :], z[:, :], ACT.Abs), t)
                t1 = AC.do(lambda e: e.activation(s1[:, :], s1[:, :], ACT.Exp, scale=-1.0), t1)
                t1 = AC.do(lambda e: e.activation(s1[:, :], s1[:, :], ACT.Ln, bias=ones[0:16, 0:1]), t1, t_ones)
                t = DV.do(lambda e: e.tensor_scalar(z[:, :], z[:, :], 0.0, None, ALU.min), t, t1)
                t = DV.do(lambda e: e.tensor_tensor(z[:, :], s1[:, :], z[:, :], ALU.subtract), t)
                t = DV.do(lambda e: e.tensor_tensor_scan(s2[:, :], onr[:, :], z[:, :], 0.0, ALU.mult, ALU.add),
                          t, t_onr)
                t = DV.do(lambda e: e.tensor_copy(c3[0:16, :], s2[:, :]), t, t_c3z)
                t = DV.do(lambda e: e.tensor_tensor(s3[:, :], s2[:, :], c3[0:16, :], ALU.subtract), t)
                t = DV.do(lambda e: e.tensor_copy(cmid[:, :], s3[:, :]), t)
                ta = DV.do(lambda e: e.tensor_copy(c3[32:48, :], cmid[:, :]), t)
                t = DV.do(lambda e: e.tensor_tensor(s3[:, :], s3[:, :], cmid[:, :], ALU.subtract), ta)
                tq["c"] = DV.do(lambda e: e.tensor_copy(c3[64:80, :], s3[:, :]), t)
                return rel

            def evac_a(m, b, tok):
                if m == 24:
                    return forget(b, tok)
                tr = need_row(r)
                rb = r["rb"]
                if m < 8:
                    t = DV.do(lambda e: e.scalar_tensor_tensor(out=qa[:, m, :], in0=b[:, :], scalar=0.125,
                                                               in1=rb[:, :], op0=ALU.mult, op1=ALU.mult), tok, tr)
                else:
                    t = DV.do(lambda e: e.tensor_tensor(ka[:, m - 8, :], b[:, :], rb[:, :], ALU.mult), tok, tr)
                tq[m] = t
                return [t]

            def evac_av(ci, tb, b, tok):
                rc = r["rc"]
                need_row(r)
                t = AC.do(lambda e: e.activation(va[:, tb, 512 * ci:512 * ci + 512], b[:, :], ACT.Copy,
                                                 scale=rc[:, tb:tb + 1]), tok, r["col"])
                tq["v"] = t
                return [t]

            lin_fm("ain", 8, [[24, 0]] + [[m] for m in range(1, 16)], rhs_x, evac_a)
            lin_tm("ain", 8, [range(16, 20), range(20, 24)], rhs_x, evac_av)
            xs_done()
            flush()
            ot = [None] * 8
            units = []
            for p in range(8):
                hold = {}
                for bi, qbs in enumerate([(0, 1), (2,), (3,)]):
                    jobs = []
                    for par in range(2):
                        h = 2 * p + par
                        segs = []
                        c0 = 0
                        for qb in qbs:
                            n = 128 * (qb + 1)
                            segs.append(dict(c0=c0, n=n, qb=qb, par=par, p=p, k=ka[:, p, 0:n],
                                             extra=[(n - 128, 128, identb[:, :], maskb[:, 0, :], None),
                                                    (0, n, sel[:, h, :], c3[:, 0:n], None)],
                                             v=[va[:, kb, 64 * h:64 * h + 64] for kb in range(qb + 1)], oc=128 * qb))
                            c0 += n
                        jobs.append(dict(par=par, segs=segs,
                                         toks=[tq[p], tq[8 + p], tq["c"], t_sel, t_idb, t_mk], vtok=tq["v"]))
                    u = dict(jobs=jobs, first=bi == 0, last=bi == 2, p=p)

                    def before(u=u, p=p, hold=hold, bi=bi):
                        if bi == 0:
                            for par in range(2):
                                hold[par] = pad_q(qz, par, qa[:, p, :], tq[p])
                        for j in u["jobs"]:
                            i, b, t = hold[j["par"]]
                            for s in j["segs"]:
                                s["q"] = b[:, 128 * s["qb"]:128 * s["qb"] + 128]
                            j["toks"] = j["toks"] + [t]

                    def after(tok, hold=hold, bi=bi):
                        if bi == 2:
                            for par in range(2):
                                qz[par].free[hold[par][0]] = [tok]
                    u["before"], u["after_scores"] = before, after
                    units.append(u)

            def oevac_a(u, pb, tok):
                p = u["p"]
                t1 = AC.do(lambda e: e.activation(xs[:, p, 0, :], pb[:, :], ACT.Copy), tok, xs_read[p])
                t2 = DV.do(lambda e: e.tensor_tensor(xs[:, p, 1, :], pb[:, :], xs[:, p, 0, :].bitcast(F32),
                                                     ALU.subtract), t1, tok, xs_read[p])
                xs_read[p] = []
                xs_tok[p] = t2
                return [t2]

            attention(units, oevac_a, c, "A_")
            fence()

        def out_proj(name, K, gain):
            r2 = rms_begin(gain)
            final = []

            def ev(m, b, tok):
                t = DV.do(lambda e: e.tensor_tensor(x[:, m, :], x[:, m, :], b[:, :], ALU.add), tok, x_tok[m])
                x_tok[m] = t
                final.append((m, t))
                return [t]
            lin_fm(name, K, DG, rhs_x, ev)
            xs_done()
            for m, t in final:
                post_x(r2, m, t)
            return r2

        r = out_proj("aout", 8, "ffn0")

        def ffn(l, kind, r, next_gain, c):
            up, dn = ("up%d" % l, "dn%d" % l) if kind == 1 else ("gu%d" % l, "sd%d" % l)
            act = sb(f"F{kind}{l}act", [128, 11, 2, S], F32R, c)
            ut = Ring([sb(f"F{kind}{l}u{i}", [128, S + 2], F32, c) for i in range(4)])
            tt = Ring([sb(f"F{kind}{l}t{i}", [128, S], F32, c) for i in range(4)])
            vv = Ring([sb(f"F{kind}{l}v{i}", [128, S], F32, c) for i in range(2)])
            for i in range(4):
                u = ut.b[i]
                ut.free[i] = [pool(lambda e, u=u: e.memset(u[:, 0:2], 0.0))]
            act_tok = [None] * 11
            act_read = [[]]
            hold = {}

            def finish(j, ta, tA, ai, ga, tG, gi):
                g = DV
                vi, v, fr = vv.get()
                t = AC.do(lambda e: e.activation(ga, ga, ACT.Silu), tG)
                t = DV.do(lambda e: e.tensor_tensor(v[:, :], ta, ga, ALU.mult), t, tA, fr)
                tt.free[ai] = [t]
                tt.free[gi] = [t]
                t2 = split_from(t, v[:, :], act, j, act_read[0])
                vv.free[vi] = [t2]
                act_tok[j] = t2

            def evac(m, b, tok):
                tr = need_row(r)
                rb = r["rb"]
                i, t_, fr2 = tt.get()
                if kind == 1:
                    ui, u, fr = ut.get()
                    t = DV.do(lambda e: e.tensor_tensor(u[:, 2:S + 2], b[:, :], rb[:, :], ALU.mult), tok, tr, fr)
                    rel = [t]
                    w = [col(f"cw{l}", 3 * m + q) for q in range(3)]
                    t = AC.do(lambda e: e.activation(t_[:, :], u[:, 2:S + 2], ACT.Identity, scale=w[2],
                                                     bias=col(f"cb{l}", m)), t, fr2, t_cf)
                    t = DV.do(lambda e: e.scalar_tensor_tensor(out=t_[:, :], in0=u[:, 1:S + 1], scalar=w[1],
                                                               in1=t_[:, :], op0=ALU.mult, op1=ALU.add), t)
                    t = DV.do(lambda e: e.scalar_tensor_tensor(out=t_[:, :], in0=u[:, 0:S], scalar=w[0],
                                                               in1=t_[:, :], op0=ALU.mult, op1=ALU.add), t)
                    ut.free[ui] = [t]
                else:
                    t = DV.do(lambda e: e.tensor_tensor(t_[:, :], b[:, :], rb[:, :], ALU.mult), tok, tr, fr2)
                    rel = [t]
                hold[m] = (t_[:, :], t, i)
                first = m < 22
                if not first:
                    j = m - 22
                    (pa, tA, ai), (pg, tG, gi) = hold[j], hold[m]
                    if kind == 2:
                        (pa, tA, ai), (pg, tG, gi) = hold[m], hold[j]
                    finish(j % 11, pa, tA, ai, pg, tG, gi)
                return rel

            def rhs_act(k):
                return act[:, k, 0, :], act[:, k, 1, :], act_tok[k]

            for h in range(2):
                lin_fm(up, 8, [[11 * h + j, 22 + 11 * h + j] for j in range(11)], rhs_x, evac)
                if h == 1:
                    xs_done()
                    r2 = rms_begin(next_gain)
                lin_fm(dn, 11, DG, rhs_act, evac_res(r2 if h else None), 11 * h)
                act_read[0] = [PE.mark()]
            return r2

        def put_pieces(dst, src, n, t1, t2, tok, bases=(0, 32, 64)):
            t = DV.do(lambda e: e.tensor_copy(dst[0:n, :], src), tok)
            t = DV.do(lambda e: e.tensor_tensor(t1[0:n, :], src, dst[0:n, :], ALU.subtract), t)
            t = DV.do(lambda e: e.tensor_copy(t2[0:n, :], t1[0:n, :]), t)
            t = DV.do(lambda e: e.tensor_copy(dst[32:32 + n, :], t2[0:n, :]), t)
            t = DV.do(lambda e: e.tensor_tensor(t1[0:n, :], t1[0:n, :], t2[0:n, :], ALU.subtract), t)
            return DV.do(lambda e: e.tensor_copy(dst[64:64 + n, :], t1[0:n, :]), t)

        def layer_b(r, c):
            qb_ = sb("B_q", [128, 12, S], F32, c)
            vb_ = sb("B_v", [128, 4, 1536], F32, c)
            stats = sb("B_stat", [128, 2, 3, 4, 8], F32, c)
            rcr = sb("B_rcr", [128, 4], F32, c)
            tq = {}
            rb, rc = r["rb"], r["rc"]

            def ev_q(m, b, tok):
                tr = need_row(r)
                tq["q", m] = DV.do(lambda e: e.scalar_tensor_tensor(out=qb_[:, m, :], in0=b[:, :], scalar=0.125,
                                                                    in1=rb[:, :], op0=ALU.mult, op1=ALU.mult),
                                   tok, tr)
                return [tq["q", m]]

            def ev_v(ci, tb, b, tok):
                s_ = rc if ci == 0 else rcr
                tq["v"] = AC.do(lambda e: e.activation(vb_[:, tb, 512 * ci:512 * ci + 512], b[:, :], ACT.Copy,
                                                       scale=s_[:, tb:tb + 1]), tok, r["col"], tq["rcr"])
                return [tq["v"]]

            lin_fm("bq", 8, [[0, 1]] + [[m] for m in range(2, 12)], rhs_x, ev_q)
            xs_done()
            for k in range(8):
                split_x(k, "kvn", x_tok[k])
            with ExitStack() as c2:
                kb_ = sb("B_k", [128, 12, S], F32, c2)

                def ev_k(m, b, tok):
                    tq["k", m] = DV.do(lambda e: e.tensor_tensor(kb_[:, m, :], b[:, :], rb[:, :], ALU.mult),
                                       tok, r["row"])
                    return [tq["k", m]]

                lin_fm("kv", 8, [[0, 1]] + [[m] for m in range(2, 12)], rhs_x, ev_k)
                b = side.get()
                for q in range(4):
                    PE.do(lambda e, q=q: e.matmul(b[1][:, q:q + 1], rb[0:1, q:S:4], ones[0:1, 0:1], start=True,
                                                  stop=True), r["row"], t_ones, b[2], inc=False)
                tp = PE.mark()
                tq["rcr"] = AC.do(lambda e: e.activation(rcr[:, :], b[1][:, 0:4], ACT.Copy), tp)
                bank_free[b[0]] = [tq["rcr"]]
                lin_tm("kv", 8, [range(12, 16), range(16, 20), range(20, 24)], rhs_x, ev_v,
                       stride=lambda ci: ci > 0)
                xs_done()
                flush()
                bias = sb("B_bias", [128, 2, 512], F32, c2)
                qz = padded(c2, "B_", 1)
                bfree = {0: [], 1: []}
                units = []
                ot = {}
                for p in range(4):
                    btok = {}
                    for g in range(3):
                        t = 4 * g + p
                        hold = {}
                        lots = [[(0, 1), (2, 3)], [(0, 1, 2, 3)], [(0, 1, 2, 3)]][g]
                        for bi, blks in enumerate(lots):
                            jobs = []
                            for par in range(2):
                                h = 2 * p + par
                                hd = 64 * (8 * g + h)
                                segs = []
                                c0 = 0
                                for b_ in blks:
                                    if g == 0:
                                        lo = max(0, b_ - 1)
                                        n = 128 * (b_ + 1 - lo)
                                        kk = kb_[:, t, 128 * lo:128 * b_ + 128]
                                        bb = bias[:, par, 256 - n:256]
                                        qs = slice(128 * b_, 128 * b_ + 128)
                                        v = [vb_[:, w, hd:hd + 64] for w in range(lo, b_ + 1)]
                                    else:
                                        n = 128
                                        kk = kb_[:, t, b_:S:4]
                                        bb = bias[:, par, 128 + 128 * g:256 + 128 * g]
                                        qs = slice(b_, S, 4)
                                        v = [vb_[:, b_, hd:hd + 64]]
                                    segs.append(dict(c0=c0, n=n, qs=qs, k=kk, bias=bb, v=v, oc=128 * b_))
                                    c0 += n
                                keep = tuple(stats[:, w, g, blks[0]:blks[-1] + 1, h] for w in range(2))
                                jobs.append(dict(par=par, segs=segs, keep=keep, toks=[tq["q", t], tq["k", t]],
                                                 vtok=tq["v"]))
                            u = dict(jobs=jobs, first=bi == 0, last=bi == len(lots) - 1, g=g, t=t)

                            def before(u=u, t=t, g=g, p=p, hold=hold, bi=bi, btok=btok):
                                if bi == 0:
                                    for par in range(2):
                                        hold[par] = pad_q(qz, par, qb_[:, t, :], tq["q", t])
                                if g < 2 and bi == 0:
                                    a0, a1 = (0, 256) if g == 0 else (256, 512)
                                    btok[g] = PO.dma(bias[:, :, a0:a1], a["biasB"][:, 2 * p:2 * p + 2, a0:a1],
                                                     dma_sem(f"bias{g}"), bfree[g])
                                for j in u["jobs"]:
                                    i, b, tk = hold[j["par"]]
                                    for s in j["segs"]:
                                        s["q"] = b[:, s["qs"]]
                                        s["btok"] = btok[min(g, 1)]
                                    j["toks"] = j["toks"] + [tk]

                            def after(tok, hold=hold, last=bi == len(lots) - 1):
                                if last:
                                    for par in range(2):
                                        qz[par].free[hold[par][0]] = [tok]

                            def after_soft(tok, g=g, bi=bi):
                                if g == 0 and bi == 1:
                                    bfree[0] = [tok]
                                if g == 2:
                                    bfree[1] = [tok]
                            u["before"], u["after_scores"], u["after_soft"] = before, after, after_soft
                            units.append(u)

                def oevac(u, pb, tok):
                    t = u["t"]
                    if u["g"] == 0:
                        ot[t] = AC.do(lambda e: e.activation(qb_[:, t, :], pb[:, :], ACT.Copy), tok)
                    else:
                        ot[t] = AC.do(lambda e: e.activation(qb_[:, t, :].rearrange("p (i r) -> p r i", r=4),
                                                             pb[:, :].rearrange("p (r i) -> p r i", r=4),
                                                             ACT.Copy), tok)
                    return [ot[t]]

                attention(units, oevac, c2, "B_")
            fence()
            ls = sb("B_ls", [8, 3, S], F32, c)
            lw = sb("B_lw", [8, 2, S], F32, c)
            l2 = sb("B_l2", [8, S], BF16, c)
            lt = sb("B_lt", [8, S], F32, c)
            a3 = [sb(f"B_a3{g}", [128, S], BF16, c) for g in range(3)]
            selp = sb("B_selp", [128, 4, 128], BF16, c)
            acc = Ring([sb(f"B_acc{i}", [128, 2, S], F32, c) for i in range(2)])
            t_sp = PO.dma(selp[:, :, :].bitcast(U16), a["selp"], dma_sem("selp"))
            tz = [pool(lambda e, g=g: e.memset(a3[g][:, :], 0.0)) for g in range(3)]
            t = (DV.sem, DV.n)
            t = AC.do(lambda e: e.activation(stats[:, 0, :, :, :], stats[:, 0, :, :, :], ACT.Ln), t)
            t = DV.do(lambda e: e.tensor_tensor(stats[:, 0, :, :, :], stats[:, 0, :, :, :], stats[:, 1, :, :, :],
                                                ALU.add), t)
            tl = []

            def lse(g):
                b, pb, fr = main.get()
                for q in range(4):
                    PE.do(lambda e, q=q: e.transpose(pb[0:8, 128 * q:128 * q + 128], stats[:, 0, g, q, :],
                                                     ident[:, :]), t, fr, inc=False)
                tp = PE.mark()
                if g == 0:
                    tl.append(AC.do(lambda e: e.activation(ls[:, g, :], pb[0:8, :], ACT.Copy), tp))
                else:
                    tl.append(AC.do(lambda e: e.activation(ls[:, g, :].rearrange("p (i r) -> p r i", r=4),
                                                           pb[0:8, :].rearrange("p (r i) -> p r i", r=4),
                                                           ACT.Copy), tp))
                bank_free[b] = [tl[-1]]
            for g in range(3):
                lse(g)
            t = DV.do(lambda e: e.tensor_tensor(lw[:, 0, :], ls[:, 0, :], ls[:, 1, :], ALU.max), tl)
            t = DV.do(lambda e: e.tensor_tensor(lw[:, 0, :], lw[:, 0, :], ls[:, 2, :], ALU.max), t)
            tg = [DV.do(lambda e, g=g: e.tensor_tensor(ls[:, g, :], ls[:, g, :], lw[:, 0, :], ALU.subtract), t)
                  for g in range(3)]
            t = AC.do(lambda e: e.activation(ls[:, :, :], ls[:, :, :], ACT.Exp), tg)
            t = DV.do(lambda e: e.tensor_tensor(lw[:, 1, :], ls[:, 0, :], ls[:, 1, :], ALU.add), t)
            t = DV.do(lambda e: e.tensor_tensor(lw[:, 1, :], lw[:, 1, :], ls[:, 2, :], ALU.add), t)
            t = DV.do(lambda e: e.reciprocal(lw[:, 0, :], lw[:, 1, :]), t)
            ta = []
            for g in range(3):
                t = DV.do(lambda e, g=g: e.tensor_tensor(ls[:, g, :], ls[:, g, :], lw[:, 0, :], ALU.mult), t)
                t = put_pieces(a3[g], ls[:, g, :], 8, lt, l2, [t, tz[g]])
                ta.append(t)

            def combine(p):
                i, ac, fr = acc.get()
                tt = None
                for g in range(3):
                    b, pb, fb = main.get()
                    tp = PE.do(lambda e, pb=pb, g=g: e.matmul(pb[:, :], selp[:, p, :], a3[g][:, :], start=True,
                                                              stop=True), ta[g], t_sp, fb)
                    o = ac[:, min(g, 1), :]
                    tm = DV.do(lambda e, pb=pb, g=g, o=o: e.tensor_tensor(o, pb[:, :], qb_[:, 4 * g + p, :],
                                                                          ALU.mult), tp, ot[4 * g + p], fr, tt)
                    bank_free[b] = [tm]
                    tt = tm
                    if g > 0:
                        tt = DV.do(lambda e: e.tensor_tensor(ac[:, 0, :], ac[:, 0, :], ac[:, 1, :], ALU.add), tm)
                xs_tok[p] = split_from(tt, ac[:, 0, :], xs, p, xs_read[p])
                acc.free[i] = [xs_tok[p]]
                xs_read[p] = []
            for p in range(4):
                combine(p)
            flush()

        def layer_e(r, c):
            rb, rc = r["rb"], r["rc"]
            qt = sb("E_q", [128, 8, S], F32, c)
            kt = sb("E_k", [128, 8, S], F32, c)
            vm = sb("E_v", [128, 4, 512], F32, c)
            r3 = sb("E_r3", [128, S], BF16, c)
            sel = sb("E_sel", [128, 16, 128], BF16, c)
            t_sel = PO.dma(sel[:, :, :].bitcast(U16), a["sel"], dma_sem("sel"))
            t_r3 = pool(lambda e: e.memset(r3[:, :], 0.0))
            tq = {}
            with ExitStack() as c1:
                u_ = sb("E_u", [128, 4, S], F32, c1)
                vg = vm
                wt = sb("E_wt", [128, 4, 128], F32, c1)
                bB = sb("E_bB", [128, 4, 128], F32, c1)
                oneh = sb("E_oneh", [128, 16, 16], F32, c1)
                rope = sb("E_rope", [128, S], F32, c1)
                gcs = [sb("E_gcs", [128, S], F32, c1), rope]
                kpe = sb("E_kpe", [128, S], F32, c1)
                cs = sb("E_cs", [128, 5, 2, S], F32R, c1)
                tmp = Ring([sb(f"E_t{i}", [128, S], F32, c1) for i in range(2)])
                sqk = Ring([sb(f"E_sqk{i}", [128, S], F32, c1) for i in range(2)])
                rbx = [sb(f"E_rb{i}", [128, S], F32, c1) for i in range(2)]
                rcx = [sb(f"E_rc{i}", [128, 8], F32, c1) for i in range(2)]
                gst = sb("E_gst", [128, 4, 12], F32, c1)
                t_wt = PO.dma(wt[:, :, :], a["gmw"], dma_sem("gmw"))
                t_bB = PO.dma(bB[:, :, :], a["gmb"], dma_sem("gmb"))
                t_oh = PO.dma(oneh[:, :, :], a["oneh"], dma_sem("oneh"))
                t_rp = PO.dma(rope[:, :], a["ropem"], dma_sem("ropem"))
                t_wt = pool(lambda e: e.memset(wt[64:128, :, 0:64], 0.0), t_wt)
                tgc = []
                for i in range(2):
                    tgc.append(DV.do(lambda e, i=i: e.tensor_scalar(gcs[i][64:128, :], rope[64:128, :],
                                                                    col("gq" if i == 0 else "gk", 0, 64, 128), None,
                                                                    ALU.mult), t_rp, t_cf, tgc))
                rn = [{"st": {}}, {"st": {}}]
                ctok = [None] * 5

                def evac(m, b, tok):
                    tr = need_row(r)
                    if m < 5:
                        w, k, K = (0, m, 3) if m < 3 else (1, m - 3, 2)
                        i, t_, fr = tmp.get()
                        t = DV.do(lambda e: e.tensor_tensor(t_[:, :], b[:, :], rb[:, :], ALU.mult), tok, tr, fr)
                        rel = [t]
                        g = col("qa", k) if w == 0 else col("kva", k)
                        t1 = AC.do(lambda e: e.activation(cs[:, m, 0, :], t_[:, :], ACT.Copy, scale=g), t)
                        t2 = DV.do(lambda e: e.scalar_tensor_tensor(out=cs[:, m, 1, :], in0=t_[:, :], scalar=g,
                                                                    in1=cs[:, m, 0, :].bitcast(F32), op0=ALU.mult,
                                                                    op1=ALU.subtract), t1)
                        ctok[m] = t2
                        sq_room()
                        ii, sq, fs = sqr.get()
                        t3 = AC.do(lambda e: e.activation(sq[:, :], t_[:, :], ACT.Square), t, fs)
                        tmp.free[i] = [t2, t3]
                        defer(stats_cols(0, k, K, sq, t3, rn[w]["st"], sqr.free[ii]), 3)
                        if k == K - 1:
                            defer(finish_stats(rn[w]["st"], 128 * K, 0, rbx[w], rcx[w], [], rn[w]), 0)
                        return rel
                    if m == 5:
                        t = DV.do(lambda e: e.tensor_tensor(kpe[64:128, :], b[64:128, :], rb[64:128, :], ALU.mult),
                                  tok, tr)
                        rel = [t]
                        for i in range(2):
                            s_ = sqk.b[i]
                            tq["sqk", i] = AC.do(lambda e, s_=s_: e.activation(s_[64:96, :], kpe[64:96, :],
                                                                               ACT.Square), t)
                        ts = [tq["sqk", 0], tq["sqk", 1]]
                        i, t_, fr = tmp.get()
                        ta = DV.do(lambda e: e.tensor_tensor(t_[64:96, :], kpe[96:128, :], gcs[1][96:128, :],
                                                             ALU.mult), t, tgc[1], fr)
                        tb_ = DV.do(lambda e: e.tensor_tensor(kpe[64:96, :], kpe[64:96, :], gcs[1][64:96, :],
                                                              ALU.mult), ts, ta)
                        tc = DV.do(lambda e: e.tensor_tensor(kpe[64:96, :], kpe[64:96, :], t_[64:96, :], ALU.add),
                                   tb_, ta)
                        tmp.free[i] = [tc]
                        tq["kpe"] = tc
                        return rel
                    j = m - 6
                    i, t_, fr = tmp.get()
                    t = DV.do(lambda e: e.tensor_tensor(t_[:, :], b[:, :], rb[:, :], ALU.mult), tok, tr, fr)
                    tq["u", j] = AC.do(lambda e: e.activation(u_[:, j, :], t_[:, :], ACT.Gelu_apprx_tanh), t)
                    tmp.free[i] = [tq["u", j]]
                    return [t]

                def evac_v(ci, tb, b, tok):
                    tq["vg", tb] = AC.do(lambda e: e.activation(vg[:, tb, :], b[:, :], ACT.Gelu_apprx_tanh,
                                                                scale=rc[:, tb:tb + 1]), tok, r["col"])
                    return [tq["vg", tb]]

                lin_fm("ei", 8, [[0, 1]] + [[m] for m in range(2, 10)], rhs_x, evac)
                lin_tm("ei", 8, [range(10, 14)], rhs_x, evac_v)
                xs_done()
                flush()

                def group_norm(tb):
                    i, t_, fr = tmp.get()
                    t = AC.do(lambda e: e.activation(t_[:, :], vg[:, tb, :], ACT.Square), tq["vg", tb], fr)
                    t = DV.do(lambda e: e.reduce_sum(gst[:, tb, 0:4], t_[:, :].rearrange("p (g c) -> p g c", g=4),
                                                     AX), t)
                    tmp.free[i] = [t]
                    t = AC.do(lambda e: e.activation(gst[:, tb, 4:8], gst[:, tb, 0:4], ACT.Sqrt, scale=1.0 / 128,
                                                     bias=col("eps")), t)
                    t = DV.do(lambda e: e.reciprocal(gst[:, tb, 8:12], gst[:, tb, 4:8]), t)
                    tq["vn", tb] = DV.do(lambda e: e.tensor_tensor(
                        vg[:, tb, :].rearrange("p (g c) -> p g c", g=4),
                        vg[:, tb, :].rearrange("p (g c) -> p g c", g=4),
                        gst[:, tb, 8:12].rearrange("p (g o) -> p g o", o=1).broadcast_to([128, 4, 128]),
                        ALU.mult), t)
                for tb in range(4):
                    group_norm(tb)
                sbank = side.get()
                nst = {"n": 0}

                def sums(sq, i, h, tok, ring):
                    n = nst["n"]
                    nst["n"] += 1
                    PE.do(lambda e: e.matmul(sbank[1][0:16, :], oneh[0:96, h, :], sq[0:96, :], start=n == 0,
                                             stop=n == 15, skip_group_check=True),
                          tok, t_oh, sbank[2] if n == 0 else None)
                    ring.free[i].append(PE.mark())
                    tq["sums"] = PE.mark()
                    norm["sq"] -= 1

                def evac_q(m, b, tok):
                    tr = need_row(rn[0])
                    t = DV.do(lambda e: e.tensor_tensor(qt[:, m, :], b[:, :], rbx[0][:, :], ALU.mult), tok, tr)
                    rel = [t]
                    sq_room()
                    i, sq, fs = sqr.get()
                    t1 = AC.do(lambda e: e.activation(sq[0:96, :], qt[0:96, m, :], ACT.Square), t, fs)
                    defer(lambda: sums(sq, i, m, t1, sqr), 3)
                    i2, t_, fr = tmp.get()
                    ta = DV.do(lambda e: e.tensor_tensor(t_[64:96, :], qt[96:128, m, :], gcs[0][96:128, :],
                                                         ALU.mult), t, tgc[0], fr)
                    tb_ = DV.do(lambda e: e.tensor_tensor(qt[64:96, m, :], qt[64:96, m, :], gcs[0][64:96, :],
                                                          ALU.mult), t1, t)
                    tq["q", m] = DV.do(lambda e: e.tensor_tensor(qt[64:96, m, :], qt[64:96, m, :], t_[64:96, :],
                                                                 ALU.add), ta, tb_)
                    tmp.free[i2] = [tq["q", m]]
                    return rel

                def evac_k(m, b, tok):
                    tr = need_row(rn[1])
                    t = DV.do(lambda e: e.tensor_tensor(kt[0:64, m, :], b[0:64, :], rbx[1][0:64, :], ALU.mult),
                              tok, tr)
                    sq_room()
                    i, sq, fs = sqk.get()
                    t1 = AC.do(lambda e: e.activation(sq[0:64, :], kt[0:64, m, :], ACT.Square), t, fs,
                               tq["sqk", i])
                    defer(lambda: sums(sq, i, 8 + m, t1, sqk), 3)
                    tq["k", m] = [t, pool(lambda e: e.tensor_copy(kt[64:96, m, :], kpe[64:96, :]), tq["kpe"])]
                    return [t]

                def evac_vm(ci, tb, b, tok):
                    tq["v"] = AC.do(lambda e: e.activation(vm[:, tb, :], b[:, :], ACT.Copy,
                                                           scale=rcx[1][:, tb:tb + 1]), tok, rn[1]["col"],
                                     tq["gates"])
                    return [tq["v"]]

                def rhs_c(o):
                    return lambda k: (cs[:, o + k, 0, :], cs[:, o + k, 1, :], ctok[o + k])

                def gate(g):
                    b, pb, fr = main.get()
                    for tb in range(4):
                        PE.do(lambda e, tb=tb: e.matmul(pb[:, 128 * tb:128 * tb + 128],
                                                        vg[:, tb, 128 * g:128 * g + 128], wt[:, g, :], start=True,
                                                        stop=True), tq["vn", tb], t_wt, fr, inc=False)
                    tp = PE.mark()
                    i, t_, fr = tmp.get()
                    t = DV.do(lambda e: e.scalar_tensor_tensor(
                        out=t_[:, :].rearrange("p (b t) -> p b t", b=4),
                        in0=pb[:, :].rearrange("p (b t) -> p b t", b=4), scalar=col("gmv", g),
                        in1=bB[:, g:g + 1, :].broadcast_to([128, 4, 128]), op0=ALU.mult, op1=ALU.add),
                        tp, fr, t_bB)
                    bank_free[b] = [t]
                    t = DV.do(lambda e: e.tensor_tensor(t_[:, :], t_[:, :], u_[:, g, :], ALU.mult), t, tq["u", g])
                    xs_tok[g] = split_from(t, t_[:, :], xs, g, xs_read[g])
                    xs_read[g] = []
                    tmp.free[i] = [xs_tok[g]]
                lin_fm("uq", 3, [[m] for m in range(8)], rhs_c(0), evac_q)
                for g in range(4):
                    gate(g)
                tq["gates"] = PE.mark()
                lin_fm("ukv", 2, [[m] for m in range(8)], rhs_c(3), evac_k)
                lin_tm("ukv", 2, [range(8, 12)], rhs_c(3), evac_vm)
                flush()

                i0, m0, f0 = tmp.get()
                i1, m1, f1 = tmp.get()
                t = AC.do(lambda e: e.activation(m0[0:16, :], sbank[1][0:16, :], ACT.Sqrt, scale=1.0 / 96,
                                                 bias=col("eps", 0, 0, 16)), tq["sums"], f0)
                bank_free[sbank[0]] = [t]
                t = DV.do(lambda e: e.reciprocal(m1[0:16, :], m0[0:16, :]), t, f1)
                t = DV.do(lambda e: e.tensor_scalar(m1[0:8, :], m1[0:8, :], 96.0 ** -0.5, None, ALU.mult), t)
                mid = kpe[0:16, 0:256].bitcast(BF16)
                t_r = put_pieces(r3, m1[0:16, :], 16, m0, mid, [t, t_r3])
                tmp.free[i0] = [t_r]
                tmp.free[i1] = [t_r]

                def scale(h, w, name):
                    b, pb, fr = main.get()
                    tp = PE.do(lambda e: e.matmul(pb[:, :], sel[:, h if name == "q" else 8 + h, :], r3[:, :],
                                                  start=True, stop=True), t_r, t_sel, fr)
                    g1 = col("gq1" if name == "q" else "gk1", 0, 0, 96)
                    tq[name + "n", h] = DV.do(lambda e: e.scalar_tensor_tensor(
                        out=w[0:96, h, :], in0=pb[0:96, :], scalar=g1, in1=w[0:96, h, :], op0=ALU.mult,
                        op1=ALU.mult), tp, tq[name, h], t_cf)
                    bank_free[b] = [tq[name + "n", h]]
                for h in range(8):
                    scale(h, qt, "q")
                    scale(h, kt, "k")
            fence()
            with ExitStack() as c1:
                units = []
                for p in range(4):
                    for bi, qbs in enumerate([(0, 1), (2,), (3,)]):
                        jobs = []
                        for par in range(2):
                            h = 2 * p + par
                            segs = []
                            c0 = 0
                            for qb in qbs:
                                n = 128 * (qb + 1)
                                segs.append(dict(c0=c0, n=n, q=qt[0:96, h, 128 * qb:128 * qb + 128],
                                                 k=kt[0:96, h, 0:n],
                                                 extra=[(n - 128, 128, identb[:, :], maskb[:, 1, :], None)],
                                                 v=[vm[:, kb, 64 * h:64 * h + 64] for kb in range(qb + 1)],
                                                 oc=128 * qb))
                                c0 += n
                            jobs.append(dict(par=par, segs=segs, toks=[tq["qn", h], tq["kn", h], t_idb, t_mk],
                                             vtok=tq["v"]))
                        units.append(dict(jobs=jobs, first=bi == 0, last=bi == 2, p=p))

                def oevac(u, pb, tok):
                    p = 4 + u["p"]
                    t1 = AC.do(lambda e: e.activation(xs[:, p, 0, :], pb[:, :], ACT.Copy), tok, xs_read[p])
                    t2 = DV.do(lambda e: e.tensor_tensor(xs[:, p, 1, :], pb[:, :], xs[:, p, 0, :].bitcast(F32),
                                                         ALU.subtract), t1, tok, xs_read[p])
                    xs_read[p] = []
                    xs_tok[p] = t2
                    return [t2]
                attention(units, oevac, c1, "E_")
            fence()

        def layer_o(r, c):
            rb, rc = r["rb"], r["rc"]
            qk = sb("O_qk", [128, 16, S], F32, c)
            rbo = [sb(f"O_rb{i}", [128, S], F32, c) for i in range(4)]
            rco = sb("O_rc", [128, 4, 8], F32, c)
            rn = [{"st": {}} for _ in range(4)]
            tq = {}
            with ExitStack() as c1:
                vo = sb("O_v", [128, 4, 2048], F32, c1)
                with ExitStack() as c2:
                    cst = sb("O_cs", [128, 2, S], F32, c2)
                    t_cs = PO.dma(cst[:, :, :], a["ropeo"], dma_sem("ropeo"))
                    tmp = Ring([sb(f"O_t{i}", [128, S], F32, c2) for i in range(4)])
                    hold = {}

                    def evac(m, b, tok):
                        tr = need_row(r)
                        t = DV.do(lambda e: e.tensor_tensor(qk[:, m, :], b[:, :], rb[:, :], ALU.mult), tok, tr)
                        rel = [t]
                        hold[m] = t
                        if m % 2:
                            x1, x2 = qk[:, m - 1, :], qk[:, m, :]
                            (i1, a1, f1), (i2, a2, f2) = tmp.get(), tmp.get()
                            co, si = cst[:, 0, :], cst[:, 1, :]
                            th = [hold[m - 1], t]
                            ta = pool(lambda e: e.tensor_tensor(a1[:, :], x2, si, ALU.mult), th, f1, t_cs)
                            tb_ = pool(lambda e: e.tensor_tensor(a2[:, :], x1, si, ALU.mult), th, f2)
                            tc = DV.do(lambda e: e.tensor_tensor(x1, x1, co, ALU.mult), tb_, t_cs)
                            td = DV.do(lambda e: e.tensor_tensor(x2, x2, co, ALU.mult), ta)
                            tq[m - 1] = DV.do(lambda e: e.tensor_tensor(x1, x1, a1[:, :], ALU.subtract), tc, ta)
                            tq[m] = DV.do(lambda e: e.tensor_tensor(x2, x2, a2[:, :], ALU.add), td, tb_)
                            tmp.free[i1] = [tq[m - 1]]
                            tmp.free[i2] = [tq[m]]
                        return rel

                    def evac_v(ci, tb, b, tok):
                        tq["v"] = AC.do(lambda e: e.activation(vo[:, tb, 512 * ci:512 * ci + 512], b[:, :],
                                                               ACT.Copy, scale=rc[:, tb:tb + 1]), tok, r["col"])
                        return [tq["v"]]
                    lin_fm("oi", 8, [[0, 1]] + [[m] for m in range(2, 16)], rhs_x, evac)
                    lin_tm("oi", 8, [range(16 + 4 * q, 20 + 4 * q) for q in range(4)], rhs_x, evac_v)
                    flush()
                fence()
                dk = sb("O_D", [128, 4, S], F32, c1)
                t_dk = PO.dma(dk[:, :, :], a["decay"], dma_sem("decay"))
                at = Ring([sb(f"O_at{i}", [128, S], F32, c1) for i in range(8)])
                sbk = Banks([0, 1])
                obk = Banks([2, 3, 4, 5])
                got = {}

                def head_scores(h):
                    got[h] = []
                    for kb in range(4):
                        n = S - 128 * kb

                        def one(kb=kb, n=n):
                            b, pb, fr = sbk.get()
                            for kk in range(2):
                                PE.do(lambda e, kk=kk: e.matmul(
                                    pb[:, 0:n], qk[:, 8 + 2 * h + kk, 128 * kb:128 * kb + 128],
                                    qk[:, 2 * h + kk, 128 * kb:S], start=kk == 0, stop=kk == 1),
                                    fr, tq[2 * h + kk], tq[8 + 2 * h + kk], inc=False)
                            tp = PE.mark()
                            i, A, fa = at.get()
                            t = DV.do(lambda e: e.tensor_tensor(A[:, 0:n], pb[:, 0:n], dk[:, h, 0:n], ALU.mult),
                                      tp, fa, t_dk)
                            bank_free[b] = [t]
                            got[h].append((i, A, t, n))
                        one()
                    tq["sc", h] = PE.mark()

                def head_pv(h):
                    bs = [obk.get() for _ in range(4)]
                    for kb in range(4):
                        i, A, t, n = got[h][kb]
                        for e_ in range(4):
                            PE.do(lambda e, kb=kb, A=A, n=n, e_=e_: e.matmul(
                                bs[e_][1][:, 128 * kb:S], vo[:, kb, 512 * h + 128 * e_:512 * h + 128 * e_ + 128],
                                A[:, 0:n], start=kb == 0, stop=kb == 3, skip_group_check=True),
                                t, bs[e_][2], tq["v"], inc=False)
                        at.free[i] = [PE.mark()]
                    tp = PE.mark()
                    for e_ in range(4):
                        def one(e_=e_):
                            o = qk[:, [2 * h, 2 * h + 1, 8 + 2 * h, 9 + 2 * h][e_], :]
                            t = AC.do(lambda e: e.activation(o, bs[e_][1][:, :], ACT.Copy), tp)
                            bank_free[bs[e_][0]] = [t]
                            tq["o", h, e_] = t
                            sq_room()
                            i, sq, fs = sqr.get()
                            t1 = AC.do(lambda e: e.activation(sq[:, :], o, ACT.Square), t, fs)
                            defer(stats_cols(0, e_, 4, sq, t1, rn[h]["st"], sqr.free[i]), 0)
                        one()
                    defer(finish_stats(rn[h]["st"], 512, 0, rbo[h], rco[:, h, :], [], rn[h]), 0)

                for h in range(5):
                    if h < 4:
                        head_scores(h)
                    if h:
                        head_pv(h - 1)
                        flush()
            fence()
            go = sb("O_go", [128, 8, 2, S], F32R, c)
            tmp = Ring([sb(f"O_u{i}", [128, S], F32, c) for i in range(4)])
            gt = [None] * 8
            gread = [[]]

            def evac_g(m, b, tok):
                f = m - 32
                h, e_, k = f // 4, f % 4, f % 8
                o = qk[:, [2 * h, 2 * h + 1, 8 + 2 * h, 9 + 2 * h][e_], :]
                i, g_, fr = tmp.get()
                t = DV.do(lambda e: e.tensor_tensor(g_[:, :], b[:, :], rb[:, :], ALU.mult), tok, fr, r["row"])
                rel = [t]
                t = AC.do(lambda e: e.activation(g_[:, :], g_[:, :], ACT.Silu), t)
                to = DV.do(lambda e: e.scalar_tensor_tensor(out=o, in0=o, scalar=col("ret", f), in1=rbo[h][:, :],
                                                            op0=ALU.mult, op1=ALU.mult),
                           tq["o", h, e_], need_row(rn[h]))
                t = DV.do(lambda e: e.tensor_tensor(g_[:, :], g_[:, :], o, ALU.mult), t, to)
                gt[k] = split_from(t, g_[:, :], go, k, gread[0])
                tmp.free[i] = [gt[k]]
                return rel

            def rhs_g(k):
                return go[:, k, 0, :], go[:, k, 1, :], gt[k]
            for h2 in range(2):
                lin_fm("oi", 8, [[32 + 8 * h2 + m] for m in range(8)], rhs_x, evac_g)
                if h2:
                    xs_done()
                r2 = rms_begin("f2_1") if h2 else None
                lin_fm("oout", 8, DG, rhs_g, evac_res(r2), 8 * h2)
                gread[0] = [PE.mark()]
            return r2

        def final_norm(r):
            flush()
            r2 = rms_begin("m2_0")
            for k in range(8):
                def one(k=k):
                    t = DV.do(lambda e: e.scalar_tensor_tensor(out=x[:, k, :], in0=x[:, k, :], scalar=col("fin", k),
                                                               in1=r["rb"][:, :], op0=ALU.mult, op1=ALU.mult),
                              r["row"], x_tok[k], norm["xread"][k])
                    x_tok[k] = t
                    post_x(r2, k, t)
                one()
            return r2

        with ExitStack() as c:
            r = ffn(0, 1, r, "mix1", c)
        fence()
        if stop >= 2:
            with ExitStack() as c:
                layer_b(r, c)
            r = out_proj("bout", 4, "ffn1")
            fence()
        if stop >= 3:
            with ExitStack() as c:
                r = ffn(1, 1, r, None, c)
            fence()
        if stop >= 4:
            r = final_norm(r)
            with ExitStack() as c:
                layer_e(r, c)
            r = out_proj("eout", 8, "f2_0")
            fence()
        if stop >= 5:
            with ExitStack() as c:
                r = ffn(0, 2, r, "m2_1", c)
            fence()
        if stop >= 6:
            with ExitStack() as c:
                r = layer_o(r, c)
            fence()
        if stop >= 7:
            with ExitStack() as c:
                r = ffn(1, 2, r, "", c)
        flush()
        outs = [SP.dma(a["out"][:, k, :], x[:, k, :], dma_sem("out"), x_tok[k]) for k in range(8)]
        SP.wait(outs[-1])

        with nc.Block() as blk:
            @blk.sync
            def _(e):
                SP.play(e)

            @blk.gpsimd
            def _(e):
                PO.play(e)

            @blk.scalar
            def _(e):
                AC.play(e)

            @blk.vector
            def _(e):
                DV.play(e)

            @blk.tensor
            def _(e):
                PE.play(e)


def host_consts():
    f = np.float32
    o = {}

    def bits(v):
        return (np.ascontiguousarray(v).view(np.uint32) >> 16).astype(np.uint16)
    o["ident"] = np.eye(128, dtype=f)
    o["identb"] = bits(np.eye(128, dtype=f))
    m = np.zeros((128, 2, 128), f)
    i = np.arange(128)
    m[:, 0, :] = np.where(i[:, None] >= i[None, :], 0.0, NEG)
    m[:, 1, :] = np.where(i[:, None] // 64 >= i[None, :] // 64, 0.0, NEG)
    o["maskb"] = bits(m)
    sel = np.zeros((128, 16, 128), f)
    for h in range(16):
        for b in (0, 32, 64):
            sel[b + h, h, :] = 1.0
    o["sel"] = bits(sel)
    selp = np.zeros((128, 4, 128), f)
    for p in range(4):
        for b in (0, 32, 64):
            selp[b + 2 * p, p, :64] = 1.0
            selp[b + 2 * p + 1, p, 64:] = 1.0
    o["selp"] = bits(selp)
    slopes = np.exp2(-8.0 * np.arange(1, 25) / 24).astype(f).reshape(3, 8)
    bias = np.full((128, 8, 512), NEG, f)
    d0 = i[:, None] + 128 - np.arange(256)[None, :]
    d1 = i[:, None] - i[None, :]
    for h in range(8):
        bias[:, h, 0:256] = np.where((d0 >= 0) & (d0 <= 128), -slopes[0, h] * d0.astype(f), NEG)
        bias[:, h, 256:384] = np.where(d1 >= 0, -slopes[1, h] * (4 * d1).astype(f), NEG)
        bias[:, h, 384:512] = np.where((d1 >= 0) & (d1 % 4 == 0), -slopes[2, h] * (4 * d1).astype(f), NEG)
    o["biasB"] = bias
    oneh = np.zeros((128, 16, 16), f)
    for h in range(16):
        oneh[:, h, h] = 1.0
    o["oneh"] = oneh

    def angles(half):
        inv = (10000.0 ** (-np.arange(half, dtype=np.float64) / half)).astype(f)
        return (np.arange(S, dtype=f)[:, None] * inv[None, :]).astype(np.float64).T
    g = angles(16)
    rp = np.zeros((128, S), f)
    rp[64:80] = rp[80:96] = np.cos(g)
    rp[96:112] = -np.sin(g)
    rp[112:128] = np.sin(g)
    o["ropem"] = rp
    g = angles(128)
    o["ropeo"] = np.stack([np.cos(g), np.sin(g)], 1).astype(f)
    lg = np.log(1.0 - 2.0 ** (-5.0 - np.arange(4))).astype(f).astype(np.float64)
    df = np.arange(S)[None, :] - i[:, None]
    o["decay"] = np.stack([np.where(df >= 0, np.exp(lg[h] * np.maximum(df, 0)) / 16.0, 0.0) for h in range(4)],
                          1).astype(f)
    return o


def cols(v):
    return np.ascontiguousarray(np.reshape(v, (-1, 128)).T)


def host_cf(i):
    cf = np.zeros((128, NCOL), np.float32)

    def put(name, v):
        c, n = COL[name]
        assert v.shape[1] == n, (name, v.shape)
        cf[:v.shape[0], c:c + n] = v
    put("mix0", cols(i["mix_norm_g"][0]))
    put("mix1", cols(i["mix_norm_g"][1]))
    put("ffn0", cols(i["ffn_norm_g"][0]))
    put("ffn1", cols(i["ffn_norm_g"][1]))
    put("kvn", cols(i["kv_norm_g"]))
    put("fin", cols(i["final_norm_g"]))
    for l in range(2):
        put(f"m2_{l}", cols(i["norm_mix_2"][l]))
        put(f"f2_{l}", cols(i["norm_ffn_2"][l]))
        cw = i["ffn_conv_w"][l].reshape(3, 44, 128)
        put(f"cw{l}", np.ascontiguousarray(cw.transpose(2, 1, 0)).reshape(128, 132))
        put(f"cb{l}", cols(i["ffn_conv_b"][l]))
    put("qa", cols(i["mla_q_a_norm_2"][0]))
    put("kva", cols(i["mla_kv_a_norm_2"][0]))
    put("gmv", cols(i["gm_v_norm_2"][0]))
    put("ret", cols(i["ret_out_norm_2"][0]))
    put("bf", i["a_b_f"][0][:, None])
    for n in ("gq", "gk"):
        g = i[f"mla_{n[1]}_norm_2"][0]
        put(n, np.concatenate([g, g[80:96], g[64:80]])[:, None])
        put(n + "1", np.concatenate([g[:64], np.ones(64, np.float32)])[:, None])
    cf[:, COL["eps"][0]] = EPS
    return cf


def matrices(i):
    z = np.zeros
    f = np.float32
    m = {}
    w = i["a_w_in"][0]
    m["ain"] = np.concatenate([w, z((D, 112), f)], 1)
    m["aout"] = i["a_w_out"][0]
    m["bq"] = i["b_w_q"][0]
    m["bout"] = i["b_w_out"][0]
    m["kv"] = i["w_kv"]
    for l in range(2):
        m[f"up{l}"], m[f"dn{l}"] = i["ffn_w_up"][l], i["ffn_w_down"][l]
        m[f"gu{l}"] = np.concatenate([i["ffn_w_gate_2"][l], i["ffn_w_up_2"][l]], 1)
        m[f"sd{l}"] = i["ffn_w_down_2"][l]
    e = i["even_w_in_2"][0]
    kp = e[:, 1664:1696]
    m["ei"] = np.concatenate([e[:, 1024:1408], e[:, 1408:1664], z((D, 64), f), kp, kp[:, 16:], kp[:, :16],
                              e[:, 0:512], e[:, 512:1024]], 1)
    uq = i["mla_w_uq_2"][0].reshape(384, 8, 96)
    m["uq"] = np.concatenate([uq, uq[:, :, 80:96], uq[:, :, 64:80]], 2).reshape(384, 1024)
    ukv = i["mla_w_ukv_2"][0].reshape(256, 8, 128)
    m["ukv"] = np.concatenate([np.concatenate([ukv[:, :, :64], z((256, 8, 64), f)], 2).reshape(256, 1024),
                               ukv[:, :, 64:].reshape(256, 512)], 1)
    m["eout"] = i["even_w_out_2"][0]
    m["oi"] = i["odd_w_in_2"][0]
    m["oout"] = i["odd_w_out_2"][0]
    return m


def host_w(i):
    plan = stream_plan()
    m = matrices(i)
    w = np.zeros((len(plan) // CT, 128, CT * 128), np.float32)
    for n, t in enumerate(plan):
        if t is not None:
            name, k, c = t
            o = n % CT * 128
            w[n // CT, :, o:o + 128] = m[name][128 * k:128 * k + 128, 128 * c:128 * c + 128]
    return w


def host_inputs(i):
    i = {k: np.asarray(v) for k, v in i.items()}
    o = host_consts()
    o["cf"] = host_cf(i)
    o["w"] = host_w(i)
    o["gmw"] = np.ascontiguousarray(i["gm_w_s_2"][0].transpose(2, 0, 1))
    o["gmb"] = np.ascontiguousarray(np.broadcast_to(i["gm_b_s_2"][0][None], (128, 4, 128)))
    o["xT"] = np.ascontiguousarray(i["x"][0].T.reshape(8, 128, S).transpose(1, 0, 2))
    return o


def kernel(**inputs):
    import concourse.bacc as bacc
    from concourse.bass_utils import run_bass_kernel_spmd

    arrays = host_inputs(inputs)
    nc = bacc.Bacc("TRN2", target_bir_lowering=False, num_devices=1)
    args = {n: nc.dram_tensor(f"in_{n}", v.shape, mybir.dt.from_np(v.dtype), kind="ExternalInput").ap()
            for n, v in arrays.items()}
    args["out"] = nc.dram_tensor("out_0", (128, 8, S), F32, kind="ExternalOutput").ap()
    build(nc, args)
    r = run_bass_kernel_spmd(nc, [{f"in_{n}": v for n, v in arrays.items()}], core_ids=[0])
    y = r.results[0]["out_0"]
    return np.ascontiguousarray(y.transpose(2, 1, 0).reshape(1, S, D))
```

```python
from contextlib import ExitStack

import numpy as np

import concourse.bass as bass
from concourse import mybir

F32 = mybir.dt.float32
F32R = mybir.dt.float32r
BF16 = mybir.dt.bfloat16
U16 = mybir.dt.uint16
ALU = mybir.AluOpType
ACT = mybir.ActivationFunctionType
AX = mybir.AxisListType.X

S = 512
D = 1024
EPS = 1e-6
NEG = -1.0e38
CT = 8
NRAW = 3
NSP = 4
NSQ = 3

_COLS = [("mix0", 8), ("ffn0", 8), ("kvn", 8), ("mix1", 8), ("ffn1", 8), ("fin", 8),
         ("m2_0", 8), ("f2_0", 8), ("m2_1", 8), ("f2_1", 8),
         ("cw0", 132), ("cb0", 44), ("cw1", 132), ("cb1", 44),
         ("qa", 3), ("kva", 2), ("gq", 1), ("gk", 1), ("gq1", 1), ("gk1", 1), ("gmv", 4), ("ret", 16), ("bf", 1), ("eps", 1)]
COL = {}
_n = 0
for _name, _k in _COLS:
    COL[_name] = (_n, _k)
    _n += _k
NCOL = _n


def stream_plan():
    out = []

    def fm(name, K, groups, k0=0):
        for g in groups:
            for k in range(K):
                for m in g:
                    out.append((name, k0 + k, m))

    def tm(name, K, cgs, k0=0):
        while len(out) % 4:
            out.append(None)
        for g in cgs:
            for k in range(K):
                for m in g:
                    out.append((name, k0 + k, m))

    def ffn(up, dn):
        for h in range(2):
            fm(up, 8, [[11 * h + j, 22 + 11 * h + j] for j in range(11)])
            fm(dn, 11, DG, 11 * h)

    fm("ain", 8, [[24, 0]] + [[m] for m in range(1, 16)])
    tm("ain", 8, [range(16, 20), range(20, 24)])
    fm("aout", 8, DG2)
    ffn("up0", "dn0")
    fm("bq", 8, [[0, 1]] + [[m] for m in range(2, 12)])
    fm("kv", 8, [[0, 1]] + [[m] for m in range(2, 12)])
    tm("kv", 8, [range(12, 16), range(16, 20), range(20, 24)])
    fm("bout", 4, DG2)
    ffn("up1", "dn1")
    fm("ei", 8, [[0, 1]] + [[m] for m in range(2, 10)])
    tm("ei", 8, [range(10, 14)])
    fm("ukv", 2, [[m] for m in range(8)])
    fm("uq", 3, [[m] for m in range(8)])
    tm("ukv", 2, [range(8, 12)])
    fm("eout", 8, DG2)
    ffn("gu0", "sd0")
    fm("oi", 8, [[0, 1]] + [[m] for m in range(2, 16)])
    tm("oi", 8, [range(16 + 4 * c, 20 + 4 * c) for c in range(4)])
    for h in range(2):
        fm("oi", 8, [[32 + 8 * h + m] for m in range(8)])
        fm("oout", 8, DG, 8 * h)
    ffn("gu1", "sd1")
    while len(out) % CT:
        out.append(None)
    return out


DG = [[0, 1], [2], [3], [4], [5], [6], [7]]
DG2 = [[0, 1, 2, 3], [4, 5, 6, 7]]


class Eng:

    def __init__(self, name, sem):
        self.name, self.sem, self.q, self.n, self.seen = name, sem, [], 0, {}

    def wait(self, *toks):
        for t in toks:
            if t is None or t[-1:] == (0,):
                continue
            if isinstance(t, list):
                self.wait(*t)
                continue
            s, v = t
            if self.seen.get(id(s), 0) < v:
                self.seen[id(s)] = v
                self.q.append(("w", s, v))

    def do(self, fn, *toks, inc=True):
        self.wait(*toks)
        rec = ["i", fn, None]
        self.q.append(rec)
        if inc:
            return self.mark()
        return None

    def mark(self):
        rec = self.q[-1]
        assert rec[0] == "i"
        if rec[2] is None:
            self.n += 1
            rec[2] = (self.sem, 1)
            self.last = (self.sem, self.n)
        return self.last

    def dma(self, out, in_, sem, *toks):
        self.wait(*toks)
        self.q.append(["i", lambda e: e.dma_start(out, in_), (sem[0], 16)])
        sem[1] += 16
        return (sem[0], sem[1])

    def play(self, e):
        for r in self.q:
            if r[0] == "w":
                e.wait_ge(r[1], r[2])
            else:
                i = r[1](e)
                if r[2]:
                    i.then_inc(*r[2])


class Ring:

    def __init__(self, bufs):
        self.b, self.free, self.i = bufs, [[] for _ in bufs], 0

    def get(self):
        i = self.i % len(self.b)
        self.i += 1
        t, self.free[i] = self.free[i], []
        return i, self.b[i], t


def build(nc, a, stop=99):
    plan = stream_plan()
    ctx = ExitStack()
    with ctx:
        def sb(name, shape, dt=F32, c=None):
            return (c or ctx).enter_context(nc.sbuf_tensor("m_" + name, shape, dt))

        def sem(name):
            return ctx.enter_context(nc.semaphore(name))

        PE, AC, DV, PO = (Eng(n, sem(f"s_{n}")) for n in ("pe", "act", "dve", "pool"))
        SP = Eng("sp", None)
        dsem = {}

        def pool(fn, *toks):
            return PO.do(fn, (PO.sem, PO.n), *toks)

        def dma_sem(name):
            if name not in dsem:
                dsem[name] = [sem(f"d_{name}"), 0]
            return dsem[name]

        ps = [ctx.enter_context(nc.psum_tensor(f"ps{i}", [128, 512], F32)) for i in range(8)]
        bank_free = [[] for _ in range(8)]

        class Banks:
            def __init__(self, ids):
                self.ids, self.i = ids, 0

            def get(self):
                b = self.ids[self.i % len(self.ids)]
                self.i += 1
                t, bank_free[b] = bank_free[b], []
                return b, ps[b], t

        main = Banks([0, 1, 2, 3, 4, 5])
        NMAIN = 6
        side = Banks([6, 7])
        tbank = Banks([4, 5])

        x = sb("x", [128, 8, S])
        xs = sb("xs", [128, 8, 2, S], F32R)
        raw = [sb(f"raw{i}", [128, CT * 128]) for i in range(NRAW)]
        wsp = [sb(f"wsp{i}", [128, 2, CT * 128], F32R) for i in range(NSP)]
        cf = sb("cf", [128, NCOL])
        ident = sb("ident", [128, 128])
        identb = sb("identb", [128, 128], BF16)
        maskb = sb("maskb", [128, 2, 128], BF16)
        ones = sb("ones", [128, 128])
        rb2 = [sb(f"rb{i}", [128, S]) for i in range(2)]
        diag = sb("diag", [128, S])
        sqr = Ring([sb(f"sq{i}", [128, S]) for i in range(NSQ)])
        rcol2 = [sb(f"rcol{i}", [128, 8]) for i in range(2)]

        gfm = sb("gfm", [128, 8])

        def col(name, i=0, p0=0, p1=128):
            if name == "fm":
                return gfm[:, i:i + 1]
            c = COL[name][0] + i
            return cf[p0:p1, c:c + 1]

        nch = len(plan) // CT
        t_cf = SP.dma(cf[:, :], a["cf"], dma_sem("cf"))
        t_x = []
        st = {"load": 0, "split": 0, "i": 0}
        raw_tok, raw_free, hi_tok, sp_tok, sp_free = {}, {}, {}, {}, {}

        def load_next():
            n = st["load"]
            if n >= nch:
                return
            st["load"] += 1
            raw_tok[n] = SP.dma(raw[n % NRAW][:, :], a["w"][n], dma_sem(f"w{n % NRAW}"), raw_free.get(n - NRAW))

        for h in range(4):
            if h < NRAW:
                load_next()
            t_x.append(SP.dma(x[:, 2 * h:2 * h + 2, :], a["xT"][:, 2 * h:2 * h + 2, :], dma_sem(f"x{h}")))
        t_id = PO.dma(ident[:, :], a["ident"], dma_sem("id"))
        t_idb = PO.dma(identb[:, :].bitcast(U16), a["identb"], dma_sem("idb"))
        t_mk = PO.dma(maskb[:, :, :].bitcast(U16), a["maskb"], dma_sem("mk"))
        t_ones = DV.do(lambda e: e.memset(ones[:, :], 1.0))
        DV.do(lambda e: e.tensor_tensor(gfm[:, :], cf[:, COL["fin"][0]:COL["fin"][0] + 8],
                                        cf[:, COL["m2_0"][0]:COL["m2_0"][0] + 8], ALU.mult), t_cf)

        def split_next():
            n = st["split"]
            st["split"] += 1
            if n < nch:
                r, w = raw[n % NRAW], wsp[n % NSP]
                hi_tok[n] = AC.do(lambda e: e.activation(w[:, 0, :], r[:, :], ACT.Copy), raw_tok[n],
                                  sp_free.get(n - NSP))
            if 0 < n <= nch:
                r1, w1 = raw[(n - 1) % NRAW], wsp[(n - 1) % NSP]
                t_lo = DV.do(lambda e: e.tensor_tensor(w1[:, 1, :], r1[:, :], w1[:, 0, :].bitcast(F32),
                                                       ALU.subtract), hi_tok[n - 1], sp_free.get(n - 1 - NSP))
                sp_tok[n - 1] = t_lo
                raw_free[n - 1] = [hi_tok[n - 1], t_lo]
                load_next()

        def use(want, n=1):
            while plan[st["i"]] is None:
                st["i"] += 1
            i = st["i"]
            c = i // CT
            if i % CT == 0 and c > 0:
                sp_free[c - 1] = PE.mark()
            while st["split"] < (min(c + NSP, nch + 1) if c else 2):
                split_next()
            assert plan[i] == want, (plan[i], want)
            st["i"] += n
            o = (i % CT) * 128
            w = wsp[c % NSP]
            return w[:, 0, o:o + 128 * n], w[:, 1, o:o + 128 * n], sp_tok[c]

        deferred = []

        def defer(fn, after=3):
            deferred.append([after, fn])

        def tick(k=1):
            for d in deferred:
                d[0] -= k
            while deferred and deferred[0][0] <= 0:
                deferred.pop(0)[1]()

        def flush():
            while deferred:
                deferred.pop(0)[1]()

        def mm3(out, lh, ll, rh, rl, first, last, *toks):
            PE.do(lambda e: e.matmul(out, lh, rh, start=first, stop=False), *toks, inc=False)
            PE.do(lambda e: e.matmul(out, lh, rl, start=False, stop=False), inc=False)
            PE.do(lambda e: e.matmul(out, ll, rh, start=False, stop=last), inc=False)

        def lin_fm(name, K, groups, rhs, evac, k0=0, banks=None, on_k=None, norm_of=None):
            late_ = []

            def out(most):
                while late_ and (norm_of is None or "row" in norm_of or len(late_) > most):
                    m, b, bank, tok = late_.pop(0)
                    bank_free[b] = evac(m, bank, tok)

            for g in groups:
                out(NMAIN - len(g))
                got = {m: (banks or main).get() for m in g}
                done = {}
                for k in range(K):
                    for m in g:
                        wh, wl, tw = use((name, k0 + k, m))
                        h, l, tr = rhs(k)
                        mm3(got[m][1][:, :], wh, wl, h, l, k == 0, k == K - 1, tw, tr, got[m][2] if k == 0 else None)
                        if k == K - 1:
                            done[m] = PE.mark()
                        tick()
                    if on_k is not None and g is groups[-1]:
                        xs_read[k] = [PE.mark()]
                        on_k(k)
                late_ += [(m, got[m][0], got[m][1], done[m]) for m in g]
                out(NMAIN)
            out(0)

        def lin_tm(name, K, cgs, lhs, evac, k0=0, stride=lambda ci: False):
            while st["i"] % 4:
                assert plan[st["i"]] is None
                st["i"] += 1
            for ci, g in enumerate(cgs):
                got = [main.get() for _ in range(4)]
                done = {}
                for k in range(K):
                    wh, wl, tw = use((name, k0 + k, g[0]), 4)
                    h, l, tr = lhs(k)
                    for tb in range(4):
                        o = slice(tb, S, 4) if stride(ci) else slice(tb * 128, tb * 128 + 128)
                        mm3(got[tb][1][:, :], h[:, o], l[:, o], wh, wl, k == 0, k == K - 1,
                            tw, tr, got[tb][2] if k == 0 else None)
                        if k == K - 1:
                            done[tb] = PE.mark()
                    tick(4)
                for tb in range(4):
                    bank_free[got[tb][0]] = evac(ci, tb, got[tb][1], done[tb])

        xs_tok = [None] * 8
        xs_read = [[] for _ in range(8)]
        norm = {"n": 0, "sq": 0, "xread": [None] * 8}

        def stats_cols(n, k, K, sq_ap, tok, st_, free):
            def fn():
                b = st_["bank"] if k else side.get()
                st_["bank"] = b
                for tb in range(4):
                    PE.do(lambda e, tb=tb: e.matmul(b[1][:, tb:tb + 1], sq_ap[:, tb * 128:tb * 128 + 128], ones[:, 0:1],
                                                    start=(k == 0 and tb == 0), stop=(k == K - 1),
                                                    skip_group_check=True),
                          tok, t_ones, b[2] if k == 0 else None, inc=False)
                free.append(PE.mark())
                norm["sq"] -= 1
            return fn

        def finish_stats(st_, dim, n, rb, rc, rb_free, out):
            def fn():
                if norm.get("row"):
                    norm["row"]()
                b = st_["bank"]
                t = AC.do(lambda e: e.activation(rc[:, 4:8], b[1][:, 0:4], ACT.Sqrt, scale=1.0 / dim, bias=col("eps")),
                          PE.mark(), t_cf, rb_free)
                bank_free[b[0]] = [t]
                t = DV.do(lambda e: e.reciprocal(rc[:, 0:4], rc[:, 4:8]), t, rb_free)
                out["col"] = t
                t = DV.do(lambda e: e.tensor_tensor(
                    diag[:, :].rearrange("p (b q) -> p b q", b=4),
                    ident[:, :].rearrange("p (o q) -> p o q", o=1).broadcast_to([128, 4, 128]),
                    rc[:, 0:4].rearrange("p (b o) -> p b o", o=1).broadcast_to([128, 4, 128]), ALU.mult),
                    t, t_id, norm.get("diag"))

                def fn2():
                    if norm["row"] is not fn2:
                        return
                    norm["row"] = None
                    c = side.get()
                    PE.do(lambda e: e.matmul(c[1][:, :], ones[:, :], diag[:, :], start=True, stop=True), t, c[2])
                    tp = norm["diag"] = PE.mark()
                    out["row"] = AC.do(lambda e: e.activation(rb[:, :], c[1][:, :], ACT.Copy), tp, rb_free)
                    bank_free[c[0]] = [out["row"]]
                norm["row"] = fn2
                defer(fn2, 6)
            return fn

        cur = {}

        def rms_begin(gain):
            n = norm["n"] = norm["n"] + 1
            r = {"st": {}, "gain": gain, "rb": rb2[n % 2], "rc": rcol2[n % 2], "n": n}
            cur["next"] = r
            return r

        def split_x(k, gain, tx):
            g = col(gain, k)
            t1 = AC.do(lambda e: e.activation(xs[:, k, 0, :], x[:, k, :], ACT.Copy, scale=g), tx, t_cf, xs_read[k])
            t2 = DV.do(lambda e: e.scalar_tensor_tensor(out=xs[:, k, 1, :], in0=x[:, k, :], scalar=g,
                                                        in1=xs[:, k, 0, :].bitcast(F32), op0=ALU.mult,
                                                        op1=ALU.subtract), t1, tx, xs_read[k])
            xs_read[k] = []
            xs_tok[k] = t2

        def sq_room(most=NSQ):
            while norm["sq"] >= most:
                deferred.pop(0)[1]()
            norm["sq"] += 1

        def post_x(r, k, tx, on_pool=False):
            if r["gain"] == "":
                return
            if r["gain"] is not None:
                split_x(k, r["gain"], tx)
            sq_room()
            i, sq, free = sqr.get()
            if on_pool:
                t = pool(lambda e: e.tensor_tensor(sq[:, :], x[:, k, :], x[:, k, :], ALU.mult), tx, free)
            else:
                t = AC.do(lambda e: e.activation(sq[:, :], x[:, k, :], ACT.Square), tx, free)
            norm["xread"][k] = t
            defer(stats_cols(0, k, 8, sq, t, r["st"], sqr.free[i]), 3)
            if k == 7:
                defer(finish_stats(r["st"], D, r["n"], r["rb"], r["rc"], r.get("free", []), r), 0)

        def rhs_x(k):
            return xs[:, k, 0, :], xs[:, k, 1, :], xs_tok[k]

        def need_row(r):
            while "row" not in r:
                flush()
            return r["row"]

        x_tok = [t_x[k // 2] for k in range(8)]

        def evac_res(r):
            def evac(m, b, tok):
                t = DV.do(lambda e: e.tensor_tensor(x[:, m, :], x[:, m, :], b[:, :], ALU.add), tok, x_tok[m])
                x_tok[m] = t
                if r is not None:
                    post_x(r, m, t)
                return [t]
            return evac

        def xs_done():
            t = PE.mark()
            for k in range(8):
                xs_read[k] = [t]

        def fence():
            toks = [PE.mark()] + [(e.sem, e.n) for e in (AC, DV, PO) if e.n]
            for e in (AC, DV, PO):
                e.wait(*toks)
            return toks

        def split_from(t_in, v, dst, k, free=None):
            t1 = AC.do(lambda e: e.activation(dst[:, k, 0, :], v, ACT.Copy), t_in, free)
            return DV.do(lambda e: e.tensor_tensor(dst[:, k, 1, :], v, dst[:, k, 0, :].bitcast(F32), ALU.subtract),
                         t1, t_in, free)

        def attention(units, oevac, c, pre, bufs=None):
            P = Ring([sb(f"{pre}P{i}", [128, S], F32, c) for i in range(6)])
            PT = Ring([sb(f"{pre}PT{i}", [128, S], F32, c) for i in range(3)])
            stt = Ring([sb(f"{pre}st{i}", [128, 16], F32, c) for i in range(6)])
            sbank = Banks([0, 1, 2, 3])
            obank = Banks([6, 7])
            ob = {}

            def scores(u):
                def one(j):
                    j["toks"] = [t() if callable(t) else t for t in j["toks"]]
                    b, pb, fr = sbank.get()
                    j["sb"] = b
                    for s in j["segs"]:
                        c0, n = s["c0"], s["n"]
                        ex = s.get("extra", [])
                        PE.do(lambda e, c0=c0, n=n, s=s: e.matmul(pb[:, c0:c0 + n], s["q"], s["k"], start=True,
                                                                  stop=not s.get("extra")), fr, j["toks"], inc=False)
                        for ei, (o, m, lt, rh, tk) in enumerate(ex):
                            PE.do(lambda e, o=o, m=m, lt=lt, rh=rh, c0=c0, z=ei == len(ex) - 1: e.matmul(
                                pb[:, c0 + o:c0 + o + m], lt, rh, start=False, stop=z),
                                tk, inc=False)
                    j["ts"] = PE.mark()
                for j in u["jobs"]:
                    one(j)
                if "after_scores" in u:
                    u["after_scores"](PE.mark())

            def soft_a(u):
                ts = []

                def top(j):
                    pb = ps[j["sb"]]
                    j["pi"], j["P"], fr = P.get()
                    j["si"], j["st"], fr2 = stt.get()
                    st_, P_ = j["st"], j["P"]
                    ns = len(j["segs"])
                    j["l"], j["mx"] = j.get("keep", (st_[:, 8:8 + ns], st_[:, 0:ns]))
                    tm = None
                    for si, s in enumerate(j["segs"]):
                        if s.get("bias") is None:
                            tm = DV.do(lambda e, si=si, s=s: e.reduce_max(j["mx"][:, si:si + 1],
                                                                          pb[:, s["c0"]:s["c0"] + s["n"]], AX),
                                       j["ts"], fr2)
                        else:
                            tm = DV.do(lambda e, si=si, s=s: e.tensor_tensor_reduce(
                                out=P_[:, s["c0"]:s["c0"] + s["n"]], in0=pb[:, s["c0"]:s["c0"] + s["n"]],
                                in1=s["bias"], scale=1.0, scalar=-3.0e38, op0=ALU.add, op1=ALU.max,
                                accum_out=j["mx"][:, si:si + 1]), j["ts"], fr2, fr, s["btok"])
                            bank_free[j["sb"]] = [tm]
                    j["fr"] = fr
                    ts.append((j, tm))

                def neg(j, tm):
                    st_, P_ = j["st"], j["P"]
                    ns = len(j["segs"])
                    tn = DV.do(lambda e: e.tensor_scalar(st_[:, 4:4 + ns], j["mx"], -1.0, None, ALU.mult), tm)
                    te = None
                    src = ps[j["sb"]] if j["segs"][0].get("bias") is None else P_
                    for si, s in enumerate(j["segs"]):
                        te = AC.do(lambda e, si=si, s=s: e.activation(
                            P_[:, s["c0"]:s["c0"] + s["n"]], src[:, s["c0"]:s["c0"] + s["n"]], ACT.Exp,
                            bias=st_[:, 4 + si:5 + si], accum_out=j["l"][:, si:si + 1]), tn, j["fr"])
                    if j["segs"][0].get("bias") is None:
                        bank_free[j["sb"]] = [te]
                    j["te"] = te
                for j in u["jobs"]:
                    top(j)
                for j, tm in ts:
                    neg(j, tm)

            def soft_b(u):
                def inv(j):
                    st_ = j["st"]
                    ns = len(j["segs"])
                    j["tr"] = DV.do(lambda e: e.reciprocal(st_[:, 12:12 + ns], j["l"]), j["te"])

                def scale(j):
                    st_, P_ = j["st"], j["P"]
                    ns = len(j["segs"])
                    if ns == 4:
                        Pv = P_[:, :].rearrange("p (s n) -> p s n", s=4)
                        tp = DV.do(lambda e: e.tensor_tensor(
                            Pv, Pv, st_[:, 12:16].rearrange("p (s o) -> p s o", o=1).broadcast_to([128, 4, 128]),
                            ALU.mult), j["tr"])
                    for si, s in enumerate(j["segs"] if ns < 4 else []):
                        tp = DV.do(lambda e, si=si, s=s: e.tensor_scalar(
                            P_[:, s["c0"]:s["c0"] + s["n"]], P_[:, s["c0"]:s["c0"] + s["n"]],
                            st_[:, 12 + si:13 + si], None, ALU.mult), j["tr"])
                    stt.free[j["si"]] = [tp]
                    j["tp"] = tp
                    j["w"] = sum(s["n"] for s in j["segs"])
                for j in u["jobs"]:
                    inv(j)
                for j in u["jobs"]:
                    scale(j)

            def transp(u):
                def one(j):
                    b, pb, fr = tbank.get()
                    P_ = j["P"]
                    for o in range(0, j["w"], 128):
                        PE.do(lambda e, o=o: e.transpose(pb[:, o:o + 128], P_[:, o:o + 128], ident[:, :]),
                              j["tp"], t_id, fr, inc=False)
                    tt = PE.mark()
                    P.free[j["pi"]] = [tt]
                    i, PT_, fr = PT.get()
                    j["PT"], j["pti"] = PT_, i
                    w = j["w"]
                    j["tpt"] = AC.do(lambda e: e.activation(PT_[:, 0:w], pb[:, 0:w], ACT.Copy), tt, fr)
                    bank_free[b] = [j["tpt"]]
                for j in u["jobs"]:
                    one(j)

            def pv(u):
                if u["first"]:
                    ob["b"] = obank.get()
                b, pb, fr = ob["b"]
                lists = []
                for j in u["jobs"]:
                    l = []
                    for s in j["segs"]:
                        nb = len(s["v"])
                        for bi, v in enumerate(s["v"]):
                            l.append((j, s["c0"] + 128 * bi, v, s["oc"], bi == 0, bi == nb - 1))
                    lists.append(l)
                for i in range(max(len(l) for l in lists)):
                    for l in lists:
                        if i < len(l):
                            j, c0, v, oc, f, z = l[i]
                            PE.do(lambda e, j=j, c0=c0, v=v, oc=oc, f=f, z=z: e.matmul(
                                pb[64 * j["par"]:64 * j["par"] + 64, oc:oc + 128], v, j["PT"][:, c0:c0 + 128],
                                start=f, stop=z), j["tpt"], j["vtok"], fr, inc=False)
                t = PE.mark()
                for j in u["jobs"]:
                    PT.free[j["pti"]] = [t]
                if u["last"]:
                    bank_free[b] = oevac(u, pb, t)

            n = len(units)
            for i in range(n + 3):
                if i < n:
                    if "before" in units[i]:
                        units[i]["before"]()
                    scores(units[i])
                    soft_a(units[i])
                    if "after_soft" in units[i]:
                        units[i]["after_soft"]((DV.sem, DV.n))
                if 1 <= i <= n:
                    soft_b(units[i - 1])
                if i >= 3:
                    pv(units[i - 3])
                if 2 <= i <= n + 1:
                    transp(units[i - 2])

        def padded(c, pre, n=2):
            bufs = [[sb(f"{pre}qz{p}{i}", [128, S], F32, c) for i in range(n)] for p in range(2)]
            rings = []
            for p in range(2):
                r = Ring(bufs[p])
                for i, b in enumerate(bufs[p]):
                    t = pool(lambda e, b=b, p=p: e.memset(b[64 * (1 - p):64 * (1 - p) + 64, :], 0.0))
                    r.free[i] = [t]
                rings.append(r)
            return rings

        def pad_q(rings, par, src, tok):
            i, b, fr = rings[par].get()
            t = pool(lambda e: e.tensor_copy(b[64 * par:64 * par + 64, :], src[64 * par:64 * par + 64, :]), tok, fr)
            return i, b, t

        r = rms_begin("mix0")

        def rhs_first(k):
            if xs_tok[k] is None:
                post_x(r, k, t_x[k // 2], on_pool=True)
            return rhs_x(k)

        with ExitStack() as c:
            qa = sb("A_q", [128, 8, S], F32, c)
            ka = sb("A_k", [128, 8, S], F32, c)
            va = sb("A_v", [128, 4, 1024], F32, c)
            c3 = sb("A_c3", [128, S], BF16, c)
            sel = sb("A_sel", [128, 16, 128], BF16, c)
            cw = [sb(f"A_cw{i}", [16, S], F32, c) for i in range(4)]
            onr = sb("A_onr", [16, S], F32, c)
            cmid = sb("A_cmid", [16, S], BF16, c)
            qz = padded(c, "A_")
            t_sel = PO.dma(sel[:, :, :].bitcast(U16), a["sel"], dma_sem("sel"))
            t_c3z = pool(lambda e: e.memset(c3[:, :], 0.0))
            t_onr = pool(lambda e: e.memset(onr[:, :], 1.0))
            tq = {}

            def forget(b, tok):
                z, s1, s2, s3 = cw
                rb = r["rb"]
                tr = need_row(r)
                t = DV.do(lambda e: e.tensor_tensor(z[:, :], b[0:16, :], rb[0:16, :], ALU.mult), tok, tr)
                rel = [t]
                t = DV.do(lambda e: e.tensor_scalar(z[:, :], z[:, :], col("bf", 0, 0, 16), None, ALU.add), t, t_cf)
                t1 = AC.do(lambda e: e.activation(s1[:, :], z[:, :], ACT.Abs), t)
                t1 = AC.do(lambda e: e.activation(s1[:, :], s1[:, :], ACT.Exp, scale=-1.0), t1)
                t1 = AC.do(lambda e: e.activation(s1[:, :], s1[:, :], ACT.Ln, bias=ones[0:16, 0:1]), t1, t_ones)
                t = DV.do(lambda e: e.tensor_scalar(z[:, :], z[:, :], 0.0, None, ALU.min), t, t1)
                t = DV.do(lambda e: e.tensor_tensor(z[:, :], s1[:, :], z[:, :], ALU.subtract), t)
                t = DV.do(lambda e: e.tensor_tensor_scan(s2[:, :], onr[:, :], z[:, :], 0.0, ALU.mult, ALU.add),
                          t, t_onr)
                t = DV.do(lambda e: e.tensor_copy(c3[0:16, :], s2[:, :]), t, t_c3z)
                t = DV.do(lambda e: e.tensor_tensor(s3[:, :], s2[:, :], c3[0:16, :], ALU.subtract), t)
                t = DV.do(lambda e: e.tensor_copy(cmid[:, :], s3[:, :]), t)
                ta = DV.do(lambda e: e.tensor_copy(c3[32:48, :], cmid[:, :]), t)
                t = DV.do(lambda e: e.tensor_tensor(s3[:, :], s3[:, :], cmid[:, :], ALU.subtract), ta)
                tq["c"] = DV.do(lambda e: e.tensor_copy(c3[64:80, :], s3[:, :]), t)
                return rel

            def evac_a(m, b, tok):
                if m == 24:
                    return forget(b, tok)
                tr = need_row(r)
                rb = r["rb"]
                if m < 8:
                    t = DV.do(lambda e: e.scalar_tensor_tensor(out=qa[:, m, :], in0=b[:, :], scalar=0.125,
                                                               in1=rb[:, :], op0=ALU.mult, op1=ALU.mult), tok, tr)
                else:
                    t = DV.do(lambda e: e.tensor_tensor(ka[:, m - 8, :], b[:, :], rb[:, :], ALU.mult), tok, tr)
                tq[m] = t
                return [t]

            def evac_av(ci, tb, b, tok):
                rc = r["rc"]
                need_row(r)
                t = AC.do(lambda e: e.activation(va[:, tb, 512 * ci:512 * ci + 512], b[:, :], ACT.Copy,
                                                 scale=rc[:, tb:tb + 1]), tok, r["col"])
                tq["v"] = t
                return [t]

            lin_fm("ain", 8, [[24, 0]] + [[m] for m in range(1, 16)], rhs_first, evac_a)
            lin_tm("ain", 8, [range(16, 20), range(20, 24)], rhs_x, evac_av)
            xs_done()
            flush()
            ot = [None] * 8
            units = []
            for p in range(8):
                hold = {}
                for bi, qbs in enumerate([(0, 1), (2,), (3,)]):
                    jobs = []
                    for par in range(2):
                        h = 2 * p + par
                        segs = []
                        c0 = 0
                        for qb in qbs:
                            n = 128 * (qb + 1)
                            segs.append(dict(c0=c0, n=n, qb=qb, par=par, p=p, k=ka[:, p, 0:n],
                                             extra=[(n - 128, 128, identb[:, :], maskb[:, 0, :], None),
                                                    (0, n, sel[:, h, :], c3[:, 0:n], None)],
                                             v=[va[:, kb, 64 * h:64 * h + 64] for kb in range(qb + 1)], oc=128 * qb))
                            c0 += n
                        jobs.append(dict(par=par, segs=segs,
                                         toks=[tq[p], tq[8 + p], tq["c"], t_sel, t_idb, t_mk], vtok=tq["v"]))
                    u = dict(jobs=jobs, first=bi == 0, last=bi == 2, p=p)

                    def before(u=u, p=p, hold=hold, bi=bi):
                        if bi == 0:
                            for par in range(2):
                                hold[par] = pad_q(qz, par, qa[:, p, :], tq[p])
                        for j in u["jobs"]:
                            i, b, t = hold[j["par"]]
                            for s in j["segs"]:
                                s["q"] = b[:, 128 * s["qb"]:128 * s["qb"] + 128]
                            j["toks"] = j["toks"] + [t]

                    def after(tok, hold=hold, bi=bi):
                        if bi == 2:
                            for par in range(2):
                                qz[par].free[hold[par][0]] = [tok]
                    u["before"], u["after_scores"] = before, after
                    units.append(u)

            def oevac_a(u, pb, tok):
                p = u["p"]
                t1 = AC.do(lambda e: e.activation(xs[:, p, 0, :], pb[:, :], ACT.Copy), tok, xs_read[p])
                t2 = DV.do(lambda e: e.tensor_tensor(xs[:, p, 1, :], pb[:, :], xs[:, p, 0, :].bitcast(F32),
                                                     ALU.subtract), t1, tok, xs_read[p])
                xs_read[p] = []
                xs_tok[p] = t2
                return [t2]

            attention(units, oevac_a, c, "A_")
            fence()

        def out_proj(name, K, gain):
            r2 = rms_begin(gain)
            final = {}

            def ev(m, b, tok):
                t = DV.do(lambda e: e.tensor_tensor(x[:, m, :], x[:, m, :], b[:, :], ALU.add), tok, x_tok[m])
                x_tok[m] = t
                final[m] = t
                if m > 3:
                    post_x(r2, m, t)
                return [t]

            def on_k(k):
                if k in (2, 3):
                    for m in (2 * k - 4, 2 * k - 3):
                        post_x(r2, m, final[m])
            lin_fm(name, K, DG2, rhs_x, ev, on_k=on_k)
            for k in range(8):
                xs_read[k] = []
            return r2

        r = out_proj("aout", 8, "ffn0")

        def ffn(l, kind, r, next_gain, c):
            up, dn = ("up%d" % l, "dn%d" % l) if kind == 1 else ("gu%d" % l, "sd%d" % l)
            act = sb(f"F{kind}{l}act", [128, 11, 2, S], F32R, c)
            ut = Ring([sb(f"F{kind}{l}u{i}", [128, S + 2], F32, c) for i in range(4)])
            tt = Ring([sb(f"F{kind}{l}t{i}", [128, S], F32, c) for i in range(4)])
            vv = Ring([sb(f"F{kind}{l}v{i}", [128, S], F32, c) for i in range(2)])
            for i in range(4):
                u = ut.b[i]
                ut.free[i] = [pool(lambda e, u=u: e.memset(u[:, 0:2], 0.0))]
            act_tok = [None] * 11
            act_read = [[]]
            hold = {}

            def finish(j, ta, tA, ai, ga, tG, gi):
                vi, v, fr = vv.get()
                t = DV.do(lambda e: e.tensor_tensor(v[:, :], ta, ga, ALU.mult), tG, tA, fr)
                tt.free[ai] = [t]
                tt.free[gi] = [t]
                t2 = split_from(t, v[:, :], act, j, act_read[0])
                vv.free[vi] = [t2]
                act_tok[j] = t2

            late = []

            def settle():
                while late:
                    finish(*late.pop(0))

            def evac(m, b, tok):
                tr = need_row(r)
                rb = r["rb"]
                i, t_, fr2 = tt.get()
                if kind == 2:
                    t = DV.do(lambda e: e.tensor_tensor(t_[:, :], b[:, :], rb[:, :], ALU.mult), tok, tr, fr2)
                    if m < 22:
                        tg = AC.do(lambda e: e.activation(t_[:, :], t_[:, :], ACT.Silu), t)
                        hold[m] = (t_[:, :], tg, i)
                    else:
                        settle()
                        pg, tG, gi = hold[m - 22]
                        late.append(((m - 22) % 11, t_[:, :], t, i, pg, tG, gi))
                    return [t]
                ui, u, fr = ut.get()
                t = DV.do(lambda e: e.tensor_tensor(u[:, 2:S + 2], b[:, :], rb[:, :], ALU.mult), tok, tr, fr)
                rel = [t]
                w = [col(f"cw{l}", 3 * m + q) for q in range(3)]
                t = AC.do(lambda e: e.activation(t_[:, :], u[:, 2:S + 2], ACT.Identity, scale=w[2],
                                                 bias=col(f"cb{l}", m)), t, fr2, t_cf)
                hold[m] = (t_, t, i, u, ui, w)
                if m < 22:
                    return rel
                settle()
                two = [hold[m - 22], hold[m]]
                ts = [q[1] for q in two]
                for tap in (1, 0):
                    for n_, (tt_, _, _, u_, _, w_) in enumerate(two):
                        ts[n_] = DV.do(lambda e, tt_=tt_, u_=u_, w_=w_, tap=tap: e.scalar_tensor_tensor(
                            out=tt_[:, :], in0=u_[:, tap:S + tap], scalar=w_[tap], in1=tt_[:, :], op0=ALU.mult,
                            op1=ALU.add), ts[n_])
                for n_ in range(2):
                    ut.free[two[n_][4]] = [ts[n_]]
                tg = AC.do(lambda e: e.activation(two[1][0][:, :], two[1][0][:, :], ACT.Silu), ts[1])
                late.append(((m - 22) % 11, two[0][0][:, :], ts[0], two[0][2], two[1][0][:, :], tg, two[1][2]))
                return rel

            def rhs_act(k):
                return act[:, k, 0, :], act[:, k, 1, :], act_tok[k]

            for h in range(2):
                lin_fm(up, 8, [[11 * h + j, 22 + 11 * h + j] for j in range(11)], rhs_x, evac, norm_of=r)
                settle()
                if h == 1:
                    xs_done()
                    r2 = rms_begin(next_gain)
                lin_fm(dn, 11, DG, rhs_act, evac_res(r2 if h else None), 11 * h)
                act_read[0] = [PE.mark()]
            return r2

        def put_pieces(dst, src, n, t1, t2, tok, bases=(0, 32, 64)):
            t = DV.do(lambda e: e.tensor_copy(dst[0:n, :], src), tok)
            t = DV.do(lambda e: e.tensor_tensor(t1[0:n, :], src, dst[0:n, :], ALU.subtract), t)
            t = DV.do(lambda e: e.tensor_copy(t2[0:n, :], t1[0:n, :]), t)
            t = DV.do(lambda e: e.tensor_copy(dst[32:32 + n, :], t2[0:n, :]), t)
            t = DV.do(lambda e: e.tensor_tensor(t1[0:n, :], t1[0:n, :], t2[0:n, :], ALU.subtract), t)
            return DV.do(lambda e: e.tensor_copy(dst[64:64 + n, :], t1[0:n, :]), t)

        def layer_b(r, c):
            qb_ = sb("B_q", [128, 12, S], F32, c)
            vb_ = sb("B_v", [128, 4, 1536], F32, c)
            stats = sb("B_stat", [128, 2, 3, 4, 8], F32, c)
            rcr = sb("B_rcr", [128, 4], F32, c)
            tq = {}
            rb, rc = r["rb"], r["rc"]

            def ev_q(m, b, tok):
                tr = need_row(r)
                tq["q", m] = DV.do(lambda e: e.scalar_tensor_tensor(out=qb_[:, m, :], in0=b[:, :], scalar=0.125,
                                                                    in1=rb[:, :], op0=ALU.mult, op1=ALU.mult),
                                   tok, tr)
                return [tq["q", m]]

            def ev_v(ci, tb, b, tok):
                s_ = rc if ci == 0 else rcr
                tq["v"] = AC.do(lambda e: e.activation(vb_[:, tb, 512 * ci:512 * ci + 512], b[:, :], ACT.Copy,
                                                       scale=s_[:, tb:tb + 1]), tok, r["col"], tq["rcr"])
                return [tq["v"]]

            lin_fm("bq", 8, [[0, 1]] + [[m] for m in range(2, 12)], rhs_x, ev_q,
                   on_k=lambda k: split_x(k, "kvn", x_tok[k]), norm_of=r)
            with ExitStack() as c2:
                kb_ = sb("B_k", [128, 12, S], F32, c2)

                def ev_k(m, b, tok):
                    tq["k", m] = DV.do(lambda e: e.tensor_tensor(kb_[:, m, :], b[:, :], rb[:, :], ALU.mult),
                                       tok, r["row"])
                    return [tq["k", m]]

                lin_fm("kv", 8, [[0, 1]] + [[m] for m in range(2, 12)], rhs_x, ev_k)
                rb_, rp_, rfree = side.get()
                for q in range(4):
                    PE.do(lambda e, q=q: e.matmul(rp_[:, q:q + 1], rb[0:1, q:S:4], ones[0:1, 0:1], start=True,
                                                  stop=True), r["row"], t_ones, rfree, inc=False)
                tp = PE.mark()
                tq["rcr"] = AC.do(lambda e: e.activation(rcr[:, :], rp_[:, 0:4], ACT.Copy), tp)
                bank_free[rb_] = [tq["rcr"]]
                lin_tm("kv", 8, [range(12, 16), range(16, 20), range(20, 24)], rhs_x, ev_v,
                       stride=lambda ci: ci > 0)
                xs_done()
                flush()
                bias = sb("B_bias", [128, 2, 512], F32, c2)
                qz = padded(c2, "B_", 1)
                bfree = {0: [], 1: []}
                units = []
                ot = {}
                for p in range(4):
                    btok = {}
                    for g in range(3):
                        t = 4 * g + p
                        hold = {}
                        lots = [[(0, 1), (2, 3)], [(0, 1, 2, 3)], [(0, 1, 2, 3)]][g]
                        for bi, blks in enumerate(lots):
                            jobs = []
                            for par in range(2):
                                h = 2 * p + par
                                hd = 64 * (8 * g + h)
                                segs = []
                                c0 = 0
                                for b_ in blks:
                                    if g == 0:
                                        lo = max(0, b_ - 1)
                                        n = 128 * (b_ + 1 - lo)
                                        kk = kb_[:, t, 128 * lo:128 * b_ + 128]
                                        bb = bias[:, par, 256 - n:256]
                                        qs = slice(128 * b_, 128 * b_ + 128)
                                        v = [vb_[:, w, hd:hd + 64] for w in range(lo, b_ + 1)]
                                    else:
                                        n = 128
                                        kk = kb_[:, t, b_:S:4]
                                        bb = bias[:, par, 128 + 128 * g:256 + 128 * g]
                                        qs = slice(b_, S, 4)
                                        v = [vb_[:, b_, hd:hd + 64]]
                                    segs.append(dict(c0=c0, n=n, qs=qs, k=kk, bias=bb, v=v, oc=128 * b_))
                                    c0 += n
                                keep = tuple(stats[:, w, g, blks[0]:blks[-1] + 1, h] for w in range(2))
                                jobs.append(dict(par=par, segs=segs, keep=keep, toks=[tq["q", t], tq["k", t]],
                                                 vtok=tq["v"]))
                            u = dict(jobs=jobs, first=bi == 0, last=bi == len(lots) - 1, g=g, t=t)

                            def before(u=u, t=t, g=g, p=p, hold=hold, bi=bi, btok=btok):
                                if bi == 0:
                                    for par in range(2):
                                        hold[par] = pad_q(qz, par, qb_[:, t, :], tq["q", t])
                                if g < 2 and bi == 0:
                                    a0, a1 = (0, 256) if g == 0 else (256, 512)
                                    btok[g] = PO.dma(bias[:, :, a0:a1], a["biasB"][:, 2 * p:2 * p + 2, a0:a1],
                                                     dma_sem(f"bias{g}"), bfree[g])
                                for j in u["jobs"]:
                                    i, b, tk = hold[j["par"]]
                                    for s in j["segs"]:
                                        s["q"] = b[:, s["qs"]]
                                        s["btok"] = btok[min(g, 1)]
                                    j["toks"] = j["toks"] + [tk]

                            def after(tok, hold=hold, last=bi == len(lots) - 1):
                                if last:
                                    for par in range(2):
                                        qz[par].free[hold[par][0]] = [tok]

                            def after_soft(tok, g=g, bi=bi):
                                if g == 0 and bi == 1:
                                    bfree[0] = [tok]
                                if g == 2:
                                    bfree[1] = [tok]
                            u["before"], u["after_scores"], u["after_soft"] = before, after, after_soft
                            units.append(u)

                def oevac(u, pb, tok):
                    t = u["t"]
                    if u["g"] == 0:
                        ot[t] = AC.do(lambda e: e.activation(qb_[:, t, :], pb[:, :], ACT.Copy), tok)
                    else:
                        ot[t] = AC.do(lambda e: e.activation(qb_[:, t, :].rearrange("p (i r) -> p r i", r=4),
                                                             pb[:, :].rearrange("p (r i) -> p r i", r=4),
                                                             ACT.Copy), tok)
                    return [ot[t]]

                attention(units, oevac, c2, "B_")
            fence()
            lse = sb("B_lse", [128, 3, 4, 8], F32, c)
            lw = sb("B_lw", [128, 3, 4, 8], F32, c)
            pc = sb("B_pc", [128, 3, 4, 96], BF16, c)
            perm = sb("B_perm", [128, 4, 4, 128], F32, c)
            a3 = [sb(f"B_a3{g}", [128, S], BF16, c) for g in range(3)]
            selp = sb("B_selp", [128, 4, 128], BF16, c)
            acc = Ring([sb(f"B_acc{i}", [128, 2, S], F32, c) for i in range(2)])
            t_sp = PO.dma(selp[:, :, :].bitcast(U16), a["selp"], dma_sem("selp"))
            t_pm = PO.dma(perm[:, :, :, :], a["perm"], dma_sem("perm"))
            tz = [pool(lambda e, g=g: e.memset(a3[g][:, :], 0.0)) for g in range(3)]
            tz.append(pool(lambda e: e.memset(pc[:, :, :, :], 0.0)))
            t = AC.do(lambda e: e.activation(stats[:, 0, :, :, :], stats[:, 0, :, :, :], ACT.Ln), (DV.sem, DV.n))
            t = DV.do(lambda e: e.tensor_tensor(lse[:, :, :, :], stats[:, 0, :, :, :], stats[:, 1, :, :, :],
                                                ALU.add), t)
            b, pb, fr = main.get()
            pbv = pb[:, 0:64].rearrange("p (b g h) -> p b g h", b=4, g=2)
            for q in range(4):
                for w in range(4):
                    PE.do(lambda e, q=q, w=w: e.matmul(pbv[:, q, :, :], perm[:, w, q, :], lse[:, 1:3, w, :],
                                                       start=w == 0, stop=w == 3), t, t_pm, fr, inc=False)
            tp = PE.mark()
            t = DV.do(lambda e: e.tensor_copy(lse[:, 1:3, :, :].rearrange("p g b h -> p b g h"), pbv), tp)
            bank_free[b] = [t]
            top = stats[:, 1, 0, :, :]
            t = DV.do(lambda e: e.tensor_tensor(top, lse[:, 0, :, :], lse[:, 1, :, :], ALU.max), t)
            t = DV.do(lambda e: e.tensor_tensor(top, top, lse[:, 2, :, :], ALU.max), t)
            tg = [DV.do(lambda e, g=g: e.tensor_tensor(lse[:, g, :, :], lse[:, g, :, :], top, ALU.subtract), t)
                  for g in range(3)]
            t = AC.do(lambda e: e.activation(lse[:, :, :, :], lse[:, :, :, :], ACT.Exp), tg)
            t = DV.do(lambda e: e.tensor_tensor(top, lse[:, 0, :, :], lse[:, 1, :, :], ALU.add), t)
            t = DV.do(lambda e: e.tensor_tensor(top, top, lse[:, 2, :, :], ALU.add), t)
            inv = stats[:, 1, 1, :, :]
            t = DV.do(lambda e: e.reciprocal(inv, top), t)
            t = [DV.do(lambda e, g=g: e.tensor_tensor(lse[:, g, :, :], lse[:, g, :, :], inv, ALU.mult), t)
                 for g in range(3)]
            t = DV.do(lambda e: e.tensor_copy(pc[:, :, :, 0:8], lse[:, :, :, :]), t, tz)
            t = DV.do(lambda e: e.tensor_tensor(lw[:, :, :, :], lse[:, :, :, :], pc[:, :, :, 0:8], ALU.subtract), t)
            t = DV.do(lambda e: e.tensor_copy(pc[:, :, :, 32:40], lw[:, :, :, :]), t)
            t = DV.do(lambda e: e.tensor_tensor(lw[:, :, :, :], lw[:, :, :, :], pc[:, :, :, 32:40], ALU.subtract), t)
            t = DV.do(lambda e: e.tensor_copy(pc[:, :, :, 64:72], lw[:, :, :, :]), t)
            ta = []

            def rows(g):
                b, pb, fr = main.get()
                pbb = pb[:, 0:256].bitcast(BF16)
                for q in range(4):
                    PE.do(lambda e, q=q: e.transpose(pbb[0:96, 128 * q:128 * q + 128], pc[:, g, q, :],
                                                     identb[:, :]), t, t_idb, fr, inc=False)
                tp = PE.mark()
                ta.append(AC.do(lambda e: e.activation(a3[g][0:96, :], pbb[0:96, :], ACT.Copy), tp, tz[g]))
                bank_free[b] = [ta[-1]]
            for g in range(3):
                rows(g)

            def combine(p):
                i, ac, fr = acc.get()
                tt = None
                for g in range(3):
                    b, pb, fb = main.get()
                    tp = PE.do(lambda e, pb=pb, g=g: e.matmul(pb[:, :], selp[:, p, :], a3[g][:, :], start=True,
                                                              stop=True), ta[g], t_sp, fb)
                    o = ac[:, min(g, 1), :]
                    tm = DV.do(lambda e, pb=pb, g=g, o=o: e.tensor_tensor(o, pb[:, :], qb_[:, 4 * g + p, :],
                                                                          ALU.mult), tp, ot[4 * g + p], fr, tt)
                    bank_free[b] = [tm]
                    tt = tm
                    if g > 0:
                        tt = DV.do(lambda e: e.tensor_tensor(ac[:, 0, :], ac[:, 0, :], ac[:, 1, :], ALU.add), tm)
                xs_tok[p] = split_from(tt, ac[:, 0, :], xs, p, xs_read[p])
                acc.free[i] = [xs_tok[p]]
                xs_read[p] = []
            for p in range(4):
                combine(p)
            flush()

        def layer_e(r, c):
            rb, rc = r["rb"], r["rc"]
            qt = sb("E_q", [128, 8, S], F32, c)
            kt = sb("E_k", [128, 8, S], F32, c)
            vm = sb("E_v", [128, 4, 512], F32, c)
            r3 = sb("E_r3", [128, S], BF16, c)
            sel = sb("E_sel", [128, 16, 128], BF16, c)
            t_sel = PO.dma(sel[:, :, :].bitcast(U16), a["sel"], dma_sem("sel"))
            t_r3 = pool(lambda e: e.memset(r3[:, :], 0.0))
            tq = {}
            with ExitStack() as c1:
                u_ = sb("E_u", [128, 4, S], F32, c1)
                vg = vm
                wt = sb("E_wt", [128, 4, 128], F32, c1)
                bB = sb("E_bB", [128, 4, 128], F32, c1)
                oneh = sb("E_oneh", [128, 16, 16], F32, c1)
                rope = sb("E_rope", [128, S], F32, c1)
                gcs = [sb("E_gcs", [128, S], F32, c1), rope]
                kpe = sb("E_kpe", [128, S], F32, c1)
                cs = sb("E_cs", [128, 5, 2, S], F32R, c1)
                tmp = Ring([sb(f"E_t{i}", [128, S], F32, c1) for i in range(2)])
                sqk = Ring([sb(f"E_sqk{i}", [128, S], F32, c1) for i in range(2)])
                rbx = [sb(f"E_rb{i}", [128, S], F32, c1) for i in range(2)]
                rcx = [sb(f"E_rc{i}", [128, 8], F32, c1) for i in range(2)]
                gst = sb("E_gst", [128, 4, 12], F32, c1)
                t_wt = PO.dma(wt[:, :, :], a["gmw"], dma_sem("gmw"))
                t_bB = PO.dma(bB[:, :, :], a["gmb"], dma_sem("gmb"))
                t_oh = PO.dma(oneh[:, :, :], a["oneh"], dma_sem("oneh"))
                t_rp = PO.dma(rope[:, :], a["ropem"], dma_sem("ropem"))
                t_wt = pool(lambda e: e.memset(wt[64:128, :, 0:64], 0.0), t_wt)
                tgc = []
                for i in range(2):
                    tgc.append(DV.do(lambda e, i=i: e.tensor_scalar(gcs[i][64:128, :], rope[64:128, :],
                                                                    col("gq" if i == 0 else "gk", 0, 64, 128), None,
                                                                    ALU.mult), t_rp, t_cf, tgc))
                rn = [{"st": {}}, {"st": {}}]
                ctok = [None] * 5

                def evac(m, b, tok):
                    tr = need_row(r)
                    if m < 5:
                        w, k, K = (0, m, 3) if m < 3 else (1, m - 3, 2)
                        i, t_, fr = tmp.get()
                        t = DV.do(lambda e: e.tensor_tensor(t_[:, :], b[:, :], rb[:, :], ALU.mult), tok, tr, fr)
                        rel = [t]
                        g = col("qa", k) if w == 0 else col("kva", k)
                        t1 = AC.do(lambda e: e.activation(cs[:, m, 0, :], t_[:, :], ACT.Copy, scale=g), t)
                        t2 = DV.do(lambda e: e.scalar_tensor_tensor(out=cs[:, m, 1, :], in0=t_[:, :], scalar=g,
                                                                    in1=cs[:, m, 0, :].bitcast(F32), op0=ALU.mult,
                                                                    op1=ALU.subtract), t1)
                        ctok[m] = t2
                        sq_room()
                        ii, sq, fs = sqr.get()
                        t3 = AC.do(lambda e: e.activation(sq[:, :], t_[:, :], ACT.Square), t, fs)
                        tmp.free[i] = [t2, t3]
                        defer(stats_cols(0, k, K, sq, t3, rn[w]["st"], sqr.free[ii]), 3)
                        if k == K - 1:
                            defer(finish_stats(rn[w]["st"], 128 * K, 0, rbx[w], rcx[w], [], rn[w]), 0)
                        return rel
                    if m == 5:
                        t = DV.do(lambda e: e.tensor_tensor(kpe[64:128, :], b[64:128, :], rb[64:128, :], ALU.mult),
                                  tok, tr)
                        rel = [t]
                        for i in range(2):
                            s_ = sqk.b[i]
                            tq["sqk", i] = AC.do(lambda e, s_=s_: e.activation(s_[64:96, :], kpe[64:96, :],
                                                                               ACT.Square), t)
                        ts = [tq["sqk", 0], tq["sqk", 1]]
                        i, t_, fr = tmp.get()
                        ta = DV.do(lambda e: e.tensor_tensor(t_[64:96, :], kpe[96:128, :], gcs[1][96:128, :],
                                                             ALU.mult), t, tgc[1], fr)
                        tb_ = DV.do(lambda e: e.tensor_tensor(kpe[64:96, :], kpe[64:96, :], gcs[1][64:96, :],
                                                              ALU.mult), ts, ta)
                        tc = DV.do(lambda e: e.tensor_tensor(kpe[64:96, :], kpe[64:96, :], t_[64:96, :], ALU.add),
                                   tb_, ta)
                        tmp.free[i] = [tc]
                        tq["kpe"] = tc
                        return rel
                    j = m - 6
                    i, t_, fr = tmp.get()
                    t = DV.do(lambda e: e.tensor_tensor(t_[:, :], b[:, :], rb[:, :], ALU.mult), tok, tr, fr)
                    tq["u", j] = AC.do(lambda e: e.activation(u_[:, j, :], t_[:, :], ACT.Gelu_apprx_tanh), t)
                    tmp.free[i] = [tq["u", j]]
                    return [t]

                def evac_v(ci, tb, b, tok):
                    tq["vg", tb] = AC.do(lambda e: e.activation(vg[:, tb, :], b[:, :], ACT.Gelu_apprx_tanh,
                                                                scale=rc[:, tb:tb + 1]), tok, r["col"])
                    return [tq["vg", tb]]

                lin_fm("ei", 8, [[0, 1]] + [[m] for m in range(2, 10)], rhs_x, evac, norm_of=r)
                lin_tm("ei", 8, [range(10, 14)], rhs_x, evac_v)
                xs_done()
                flush()

                def group_norm(tb):
                    i, t_, fr = tmp.get()
                    t = AC.do(lambda e: e.activation(t_[:, :], vg[:, tb, :], ACT.Square), tq["vg", tb], fr)
                    t = DV.do(lambda e: e.reduce_sum(gst[:, tb, 0:4], t_[:, :].rearrange("p (g c) -> p g c", g=4),
                                                     AX), t)
                    tmp.free[i] = [t]
                    t = AC.do(lambda e: e.activation(gst[:, tb, 4:8], gst[:, tb, 0:4], ACT.Sqrt, scale=1.0 / 128,
                                                     bias=col("eps")), t)
                    t = DV.do(lambda e: e.reciprocal(gst[:, tb, 8:12], gst[:, tb, 4:8]), t)
                    tq["vn", tb] = DV.do(lambda e: e.tensor_tensor(
                        vg[:, tb, :].rearrange("p (g c) -> p g c", g=4),
                        vg[:, tb, :].rearrange("p (g c) -> p g c", g=4),
                        gst[:, tb, 8:12].rearrange("p (g o) -> p g o", o=1).broadcast_to([128, 4, 128]),
                        ALU.mult), t)
                sbank = side.get()
                nst = {"n": 0}

                def sums(sq, i, h, tok, ring):
                    n = nst["n"]
                    nst["n"] += 1
                    PE.do(lambda e: e.matmul(sbank[1][0:16, :], oneh[0:96, h, :], sq[0:96, :], start=n == 0,
                                             stop=n == 15, skip_group_check=True),
                          tok, t_oh, sbank[2] if n == 0 else None)
                    ring.free[i].append(PE.mark())
                    tq["sums"] = PE.mark()
                    norm["sq"] -= 1

                def evac_q(m, b, tok):
                    tr = need_row(rn[0])
                    t = DV.do(lambda e: e.tensor_tensor(qt[:, m, :], b[:, :], rbx[0][:, :], ALU.mult), tok, tr)
                    rel = [t]
                    sq_room()
                    i, sq, fs = sqr.get()
                    t1 = AC.do(lambda e: e.activation(sq[0:96, :], qt[0:96, m, :], ACT.Square), t, fs)
                    defer(lambda: sums(sq, i, m, t1, sqr), 3)
                    i2, t_, fr = tmp.get()
                    ta = DV.do(lambda e: e.tensor_tensor(t_[64:96, :], qt[96:128, m, :], gcs[0][96:128, :],
                                                         ALU.mult), t, tgc[0], fr)
                    tb_ = DV.do(lambda e: e.tensor_tensor(qt[64:96, m, :], qt[64:96, m, :], gcs[0][64:96, :],
                                                          ALU.mult), t1, t)
                    tq["q", m] = DV.do(lambda e: e.tensor_tensor(qt[64:96, m, :], qt[64:96, m, :], t_[64:96, :],
                                                                 ALU.add), ta, tb_)
                    tmp.free[i2] = [tq["q", m]]
                    return rel

                def evac_k(m, b, tok):
                    tr = need_row(rn[1])
                    t = DV.do(lambda e: e.tensor_tensor(kt[0:64, m, :], b[0:64, :], rbx[1][0:64, :], ALU.mult),
                              tok, tr)
                    if m % 2:
                        group_norm(m // 2)
                    sq_room(2)
                    i, sq, fs = sqk.get()
                    t1 = AC.do(lambda e: e.activation(sq[0:64, :], kt[0:64, m, :], ACT.Square), t, fs,
                               tq["sqk", i])
                    defer(lambda: sums(sq, i, 8 + m, t1, sqk), 3)
                    tq["k", m] = [t, pool(lambda e: e.tensor_copy(kt[64:96, m, :], kpe[64:96, :]), tq["kpe"])]
                    return [t]

                def evac_vm(ci, tb, b, tok):
                    tq["v"] = AC.do(lambda e: e.activation(vm[:, tb, :], b[:, :], ACT.Copy,
                                                           scale=rcx[1][:, tb:tb + 1]), tok, rn[1]["col"],
                                     tq["gates"])
                    return [tq["v"]]

                def rhs_c(o):
                    return lambda k: (cs[:, o + k, 0, :], cs[:, o + k, 1, :], ctok[o + k])

                def gate(g):
                    b, pb, fr = main.get()
                    for tb in range(4):
                        PE.do(lambda e, tb=tb: e.matmul(pb[:, 128 * tb:128 * tb + 128],
                                                        vg[:, tb, 128 * g:128 * g + 128], wt[:, g, :], start=True,
                                                        stop=True), tq["vn", tb], t_wt, fr, inc=False)
                    tp = PE.mark()
                    i, t_, fr = tmp.get()
                    t = DV.do(lambda e: e.scalar_tensor_tensor(
                        out=t_[:, :].rearrange("p (b t) -> p b t", b=4),
                        in0=pb[:, :].rearrange("p (b t) -> p b t", b=4), scalar=col("gmv", g),
                        in1=bB[:, g:g + 1, :].broadcast_to([128, 4, 128]), op0=ALU.mult, op1=ALU.add),
                        tp, fr, t_bB)
                    bank_free[b] = [t]
                    t = DV.do(lambda e: e.tensor_tensor(t_[:, :], t_[:, :], u_[:, g, :], ALU.mult), t, tq["u", g])
                    xs_tok[g] = split_from(t, t_[:, :], xs, g, xs_read[g])
                    xs_read[g] = []
                    tmp.free[i] = [xs_tok[g]]
                lin_fm("ukv", 2, [[m] for m in range(8)], rhs_c(3), evac_k)
                lin_fm("uq", 3, [[m] for m in range(8)], rhs_c(0), evac_q)
                flush()

                i0, m0, f0 = tmp.get()
                i1, m1, f1 = tmp.get()
                t = AC.do(lambda e: e.activation(m0[0:16, :], sbank[1][0:16, :], ACT.Sqrt, scale=1.0 / 96,
                                                 bias=col("eps", 0, 0, 16)), tq["sums"], f0)
                bank_free[sbank[0]] = [t]
                t = DV.do(lambda e: e.reciprocal(m1[0:16, :], m0[0:16, :]), t, f1)
                t = DV.do(lambda e: e.tensor_scalar(m1[0:8, :], m1[0:8, :], 96.0 ** -0.5, None, ALU.mult), t)
                mid = kpe[0:16, 0:256].bitcast(BF16)
                t_r = put_pieces(r3, m1[0:16, :], 16, m0, mid, [t, t_r3])
                tmp.free[i0] = [t_r]
                tmp.free[i1] = [t_r]

                for g in range(4):
                    gate(g)
                tq["gates"] = PE.mark()
                lin_tm("ukv", 2, [range(8, 12)], rhs_c(3), evac_vm)
                tq["r"] = t_r
            flush()
            fence()
            with ExitStack() as c1:
                def scale(h, w, name):
                    b, pb, fr = tbank.get()
                    tp = PE.do(lambda e: e.matmul(pb[:, :], sel[:, h if name == "q" else 8 + h, :], r3[:, :],
                                                  start=True, stop=True), tq["r"], t_sel, fr)
                    g1 = col("gq1" if name == "q" else "gk1", 0, 0, 96)
                    tq[name + "n", h] = DV.do(lambda e: e.scalar_tensor_tensor(
                        out=w[0:96, h, :], in0=pb[0:96, :], scalar=g1, in1=w[0:96, h, :], op0=ALU.mult,
                        op1=ALU.mult), tp, tq[name, h], t_cf)
                    bank_free[b] = [tq[name + "n", h]]
                for h in range(2):
                    scale(h, qt, "q")
                    scale(h, kt, "k")
                units = []
                for p in range(4):
                    for bi, qbs in enumerate([(0, 1), (2,), (3,)]):
                        jobs = []
                        for par in range(2):
                            h = 2 * p + par
                            segs = []
                            c0 = 0
                            for qb in qbs:
                                n = 128 * (qb + 1)
                                segs.append(dict(c0=c0, n=n, q=qt[0:96, h, 128 * qb:128 * qb + 128],
                                                 k=kt[0:96, h, 0:n],
                                                 extra=[(n - 128, 128, identb[:, :], maskb[:, 1, :], None)],
                                                 v=[vm[:, kb, 64 * h:64 * h + 64] for kb in range(qb + 1)],
                                                 oc=128 * qb))
                                c0 += n
                            jobs.append(dict(par=par, segs=segs, toks=[lambda h=h: tq["qn", h], lambda h=h: tq["kn", h], t_idb, t_mk],
                                             vtok=tq["v"]))
                        def before(p=p, bi=bi):
                            if bi == 2 and p < 3:
                                for h in (2 * p + 2, 2 * p + 3):
                                    scale(h, qt, "q")
                                    scale(h, kt, "k")
                        units.append(dict(jobs=jobs, first=bi == 0, last=bi == 2, p=p, before=before))

                def oevac(u, pb, tok):
                    p = 4 + u["p"]
                    t1 = AC.do(lambda e: e.activation(xs[:, p, 0, :], pb[:, :], ACT.Copy), tok, xs_read[p])
                    t2 = DV.do(lambda e: e.tensor_tensor(xs[:, p, 1, :], pb[:, :], xs[:, p, 0, :].bitcast(F32),
                                                         ALU.subtract), t1, tok, xs_read[p])
                    xs_read[p] = []
                    xs_tok[p] = t2
                    return [t2]
                attention(units, oevac, c1, "E_")
            fence()

        def layer_o(r, c):
            rb, rc = r["rb"], r["rc"]
            qk = sb("O_qk", [128, 16, S], F32, c)
            rbo = [sb(f"O_rb{i}", [128, S], F32, c) for i in range(4)]
            rco = sb("O_rc", [128, 4, 8], F32, c)
            rn = [{"st": {}} for _ in range(4)]
            tq = {}
            with ExitStack() as c1:
                vo = sb("O_v", [128, 4, 2048], F32, c1)
                with ExitStack() as c2:
                    cst = sb("O_cs", [128, 2, S], F32, c2)
                    t_cs = PO.dma(cst[:, :, :], a["ropeo"], dma_sem("ropeo"))
                    tmp = Ring([sb(f"O_t{i}", [128, S], F32, c2) for i in range(4)])
                    hold = {}

                    def evac(m, b, tok):
                        tr = need_row(r)
                        t = DV.do(lambda e: e.tensor_tensor(qk[:, m, :], b[:, :], rb[:, :], ALU.mult), tok, tr)
                        rel = [t]
                        hold[m] = t
                        if m % 2:
                            x1, x2 = qk[:, m - 1, :], qk[:, m, :]
                            (i1, a1, f1), (i2, a2, f2) = tmp.get(), tmp.get()
                            co, si = cst[:, 0, :], cst[:, 1, :]
                            th = [hold[m - 1], t]
                            ta = pool(lambda e: e.tensor_tensor(a1[:, :], x2, si, ALU.mult), th, f1, t_cs)
                            tb_ = pool(lambda e: e.tensor_tensor(a2[:, :], x1, si, ALU.mult), th, f2)
                            tc = DV.do(lambda e: e.tensor_tensor(x1, x1, co, ALU.mult), tb_, t_cs)
                            td = DV.do(lambda e: e.tensor_tensor(x2, x2, co, ALU.mult), ta)
                            tq[m - 1] = DV.do(lambda e: e.tensor_tensor(x1, x1, a1[:, :], ALU.subtract), tc, ta)
                            tq[m] = DV.do(lambda e: e.tensor_tensor(x2, x2, a2[:, :], ALU.add), td, tb_)
                            tmp.free[i1] = [tq[m - 1]]
                            tmp.free[i2] = [tq[m]]
                        return rel

                    def evac_v(ci, tb, b, tok):
                        tq["v"] = AC.do(lambda e: e.activation(vo[:, tb, 512 * ci:512 * ci + 512], b[:, :],
                                                               ACT.Copy, scale=rc[:, tb:tb + 1]), tok, r["col"])
                        return [tq["v"]]
                    lin_fm("oi", 8, [[0, 1]] + [[m] for m in range(2, 16)], rhs_x, evac, norm_of=r)
                    lin_tm("oi", 8, [range(16 + 4 * q, 20 + 4 * q) for q in range(4)], rhs_x, evac_v)
                    flush()
                fence()
                dk = sb("O_D", [128, 4, S], F32, c1)
                t_dk = PO.dma(dk[:, :, :], a["decay"], dma_sem("decay"))
                at = Ring([sb(f"O_at{i}", [128, S], F32, c1) for i in range(8)])
                hsum = Ring([sb(f"O_h{i}", [128, S], F32, c1) for i in range(2)])
                sbk = Banks([0, 1])
                obk = Banks([2, 3, 4, 5])
                got = {}

                def head_scores(h):
                    got[h] = []
                    for kb in range(4):
                        n = S - 128 * kb

                        def one(kb=kb, n=n):
                            b, pb, fr = sbk.get()
                            for kk in range(2):
                                PE.do(lambda e, kk=kk: e.matmul(
                                    pb[:, 0:n], qk[:, 8 + 2 * h + kk, 128 * kb:128 * kb + 128],
                                    qk[:, 2 * h + kk, 128 * kb:S], start=kk == 0, stop=kk == 1),
                                    fr, tq[2 * h + kk], tq[8 + 2 * h + kk], inc=False)
                            tp = PE.mark()
                            i, A, fa = at.get()
                            t = DV.do(lambda e: e.tensor_tensor(A[:, 0:n], pb[:, 0:n], dk[:, h, 0:n], ALU.mult),
                                      tp, fa, t_dk)
                            bank_free[b] = [t]
                            got[h].append((i, A, t, n))
                        one()
                    tq["sc", h] = PE.mark()

                def head_pv(h):
                    bs = [obk.get() for _ in range(4)]
                    for kb in range(4):
                        i, A, t, n = got[h][kb]
                        for e_ in range(4):
                            PE.do(lambda e, kb=kb, A=A, n=n, e_=e_: e.matmul(
                                bs[e_][1][:, 128 * kb:S], vo[:, kb, 512 * h + 128 * e_:512 * h + 128 * e_ + 128],
                                A[:, 0:n], start=kb == 0, stop=kb == 3, skip_group_check=True),
                                t, bs[e_][2], tq["v"], inc=False)
                        at.free[i] = [PE.mark()]
                    tp = PE.mark()
                    hs = {}
                    hs["ia"], hs["a"], hs["fa"] = hsum.get()
                    hs["ib"], hs["b"], hs["fb"] = sqr.get()
                    for e_ in range(4):
                        def one(e_=e_, hs=hs):
                            o = qk[:, [2 * h, 2 * h + 1, 8 + 2 * h, 9 + 2 * h][e_], :]
                            t = AC.do(lambda e: e.activation(o, bs[e_][1][:, :], ACT.Copy), tp)
                            bank_free[bs[e_][0]] = [t]
                            tq["o", h, e_] = t
                            if e_ == 0:
                                hs["t"] = pool(lambda e: e.tensor_tensor(hs["a"][:, :], o, o, ALU.mult), t, hs["fa"])
                            else:
                                t1 = pool(lambda e: e.tensor_tensor(hs["b"][:, :], o, o, ALU.mult), t, hs["fb"])
                                hs["t"] = pool(lambda e: e.tensor_tensor(hs["a"][:, :], hs["a"][:, :],
                                                                         hs["b"][:, :], ALU.add), t1)
                        one()
                    sqr.free[hs["ib"]] = [hs["t"]]
                    norm["sq"] += 1
                    defer(stats_cols(0, 0, 1, hs["a"], hs["t"], rn[h]["st"], hsum.free[hs["ia"]]), 14)
                    defer(finish_stats(rn[h]["st"], 512, 0, rbo[h], rco[:, h, :], [], rn[h]), 0)

                for h in range(5):
                    if h < 4:
                        head_scores(h)
                    early = len(deferred)
                    if h:
                        head_pv(h - 1)
                    for _ in range(early):
                        deferred.pop(0)[1]()
            fence()
            go = sb("O_go", [128, 8, 2, S], F32R, c)
            tmp = Ring([sb(f"O_u{i}", [128, S], F32, c) for i in range(4)])
            gt = [None] * 8
            gread = [[]]

            def evac_g(m, b, tok):
                f = m - 32
                h, e_, k = f // 4, f % 4, f % 8
                o = qk[:, [2 * h, 2 * h + 1, 8 + 2 * h, 9 + 2 * h][e_], :]
                i, g_, fr = tmp.get()
                t = DV.do(lambda e: e.tensor_tensor(g_[:, :], b[:, :], rb[:, :], ALU.mult), tok, fr, r["row"])
                rel = [t]
                t = AC.do(lambda e: e.activation(g_[:, :], g_[:, :], ACT.Silu), t)
                to = DV.do(lambda e: e.scalar_tensor_tensor(out=o, in0=o, scalar=col("ret", f), in1=rbo[h][:, :],
                                                            op0=ALU.mult, op1=ALU.mult),
                           tq["o", h, e_], need_row(rn[h]))
                t = DV.do(lambda e: e.tensor_tensor(g_[:, :], g_[:, :], o, ALU.mult), t, to)
                gt[k] = split_from(t, g_[:, :], go, k, gread[0])
                tmp.free[i] = [gt[k]]
                return rel

            def rhs_g(k):
                return go[:, k, 0, :], go[:, k, 1, :], gt[k]
            for h2 in range(2):
                lin_fm("oi", 8, [[32 + 8 * h2 + m] for m in range(8)], rhs_x, evac_g)
                if h2:
                    xs_done()
                r2 = rms_begin("f2_1") if h2 else None
                lin_fm("oout", 8, DG, rhs_g, evac_res(r2), 8 * h2)
                gread[0] = [PE.mark()]
            return r2

        def final_norm(r):
            r2 = rms_begin("m2_0")
            sub = {}

            def both():
                t = DV.do(lambda e: e.tensor_tensor(r2["rb"][:, :], r2["rb"][:, :], r["rb"][:, :], ALU.mult),
                          sub["row"], r["row"])
                r2["col"] = DV.do(lambda e: e.tensor_tensor(r2["rc"][:, 0:4], r2["rc"][:, 0:4], r["rc"][:, 0:4],
                                                            ALU.mult), sub["row"], sub["col"], r["col"])
                r2["row"] = t

            def renew():
                if "row" not in r:
                    defer(renew, 1)
                    return

                def one(k):
                    t = DV.do(lambda e: e.scalar_tensor_tensor(out=x[:, k, :], in0=x[:, k, :], scalar=col("fin", k),
                                                               in1=r["rb"][:, :], op0=ALU.mult, op1=ALU.mult),
                              r["row"], x_tok[k], norm["xread"][k])
                    x_tok[k] = t
                    sq_room()
                    i, sq, free = sqr.get()
                    t = AC.do(lambda e: e.activation(sq[:, :], x[:, k, :], ACT.Square), t, free)
                    if k < 7:
                        defer(lambda: one(k + 1), 2)
                    defer(stats_cols(0, k, 8, sq, t, r2["st"], sqr.free[i]), 4)
                    if k == 7:
                        defer(finish_stats(r2["st"], D, 0, r2["rb"], r2["rc"], [], sub), 0)
                        defer(tail, 4)

                def tail():
                    if "row" not in sub:
                        defer(tail, 1)
                        return
                    both()
                one(0)
            defer(renew, 1)
            return r2

        with ExitStack() as c:
            r = ffn(0, 1, r, "mix1", c)
        fence()
        if stop >= 2:
            with ExitStack() as c:
                layer_b(r, c)
            r = out_proj("bout", 4, "ffn1")
            fence()
        if stop >= 3:
            with ExitStack() as c:
                r = ffn(1, 1, r, "fm", c)
            fence()
        if stop >= 4:
            r = final_norm(r)
            with ExitStack() as c:
                layer_e(r, c)
            r = out_proj("eout", 8, "f2_0")
            fence()
        if stop >= 5:
            with ExitStack() as c:
                r = ffn(0, 2, r, "m2_1", c)
            fence()
        if stop >= 6:
            with ExitStack() as c:
                r = layer_o(r, c)
            fence()
        if stop >= 7:
            with ExitStack() as c:
                r = ffn(1, 2, r, "", c)
        flush()
        outs = [SP.dma(a["out"][:, k, :], x[:, k, :], dma_sem("out"), x_tok[k]) for k in range(8)]
        SP.wait(outs[-1])

        with nc.Block() as blk:
            @blk.sync
            def _(e):
                SP.play(e)

            @blk.gpsimd
            def _(e):
                PO.play(e)

            @blk.scalar
            def _(e):
                AC.play(e)

            @blk.vector
            def _(e):
                DV.play(e)

            @blk.tensor
            def _(e):
                PE.play(e)


def host_consts():
    f = np.float32
    o = {}

    def bits(v):
        return (np.ascontiguousarray(v).view(np.uint32) >> 16).astype(np.uint16)
    o["ident"] = np.eye(128, dtype=f)
    o["identb"] = bits(np.eye(128, dtype=f))
    m = np.zeros((128, 2, 128), f)
    i = np.arange(128)
    m[:, 0, :] = np.where(i[:, None] >= i[None, :], 0.0, NEG)
    m[:, 1, :] = np.where(i[:, None] // 64 >= i[None, :] // 64, 0.0, NEG)
    o["maskb"] = bits(m)
    sel = np.zeros((128, 16, 128), f)
    for h in range(16):
        for b in (0, 32, 64):
            sel[b + h, h, :] = 1.0
    o["sel"] = bits(sel)
    selp = np.zeros((128, 4, 128), f)
    for p in range(4):
        for b in (0, 32, 64):
            selp[b + 2 * p, p, :64] = 1.0
            selp[b + 2 * p + 1, p, 64:] = 1.0
    o["selp"] = bits(selp)
    slopes = np.exp2(-8.0 * np.arange(1, 25) / 24).astype(f).reshape(3, 8)
    bias = np.full((128, 8, 512), NEG, f)
    d0 = i[:, None] + 128 - np.arange(256)[None, :]
    d1 = i[:, None] - i[None, :]
    for h in range(8):
        bias[:, h, 0:256] = np.where((d0 >= 0) & (d0 <= 128), -slopes[0, h] * d0.astype(f), NEG)
        bias[:, h, 256:384] = np.where(d1 >= 0, -slopes[1, h] * (4 * d1).astype(f), NEG)
        bias[:, h, 384:512] = np.where((d1 >= 0) & (d1 % 4 == 0), -slopes[2, h] * (4 * d1).astype(f), NEG)
    o["biasB"] = bias
    perm = np.zeros((128, 4, 4, 128), f)
    for w in range(4):
        for t in range(w, S, 4):
            perm[t // 4, w, t // 128, t % 128] = 1.0
    o["perm"] = perm
    oneh = np.zeros((128, 16, 16), f)
    for h in range(16):
        oneh[:, h, h] = 1.0
    o["oneh"] = oneh

    def angles(half):
        inv = (10000.0 ** (-np.arange(half, dtype=np.float64) / half)).astype(f)
        return (np.arange(S, dtype=f)[:, None] * inv[None, :]).astype(np.float64).T
    g = angles(16)
    rp = np.zeros((128, S), f)
    rp[64:80] = rp[80:96] = np.cos(g)
    rp[96:112] = -np.sin(g)
    rp[112:128] = np.sin(g)
    o["ropem"] = rp
    g = angles(128)
    o["ropeo"] = np.stack([np.cos(g), np.sin(g)], 1).astype(f)
    lg = np.log(1.0 - 2.0 ** (-5.0 - np.arange(4))).astype(f).astype(np.float64)
    df = np.arange(S)[None, :] - i[:, None]
    o["decay"] = np.stack([np.where(df >= 0, np.exp(lg[h] * np.maximum(df, 0)) / 16.0, 0.0) for h in range(4)],
                          1).astype(f)
    return o


def cols(v):
    return np.ascontiguousarray(np.reshape(v, (-1, 128)).T)


def host_cf(i):
    cf = np.zeros((128, NCOL), np.float32)

    def put(name, v):
        c, n = COL[name]
        assert v.shape[1] == n, (name, v.shape)
        cf[:v.shape[0], c:c + n] = v
    put("mix0", cols(i["mix_norm_g"][0]))
    put("mix1", cols(i["mix_norm_g"][1]))
    put("ffn0", cols(i["ffn_norm_g"][0]))
    put("ffn1", cols(i["ffn_norm_g"][1]))
    put("kvn", cols(i["kv_norm_g"]))
    put("fin", cols(i["final_norm_g"]))
    for l in range(2):
        put(f"m2_{l}", cols(i["norm_mix_2"][l]))
        put(f"f2_{l}", cols(i["norm_ffn_2"][l]))
        cw = i["ffn_conv_w"][l].reshape(3, 44, 128)
        put(f"cw{l}", np.ascontiguousarray(cw.transpose(2, 1, 0)).reshape(128, 132))
        put(f"cb{l}", cols(i["ffn_conv_b"][l]))
    put("qa", cols(i["mla_q_a_norm_2"][0]))
    put("kva", cols(i["mla_kv_a_norm_2"][0]))
    put("gmv", cols(i["gm_v_norm_2"][0]))
    put("ret", cols(i["ret_out_norm_2"][0]))
    put("bf", i["a_b_f"][0][:, None])
    for n in ("gq", "gk"):
        g = i[f"mla_{n[1]}_norm_2"][0]
        put(n, np.concatenate([g, g[80:96], g[64:80]])[:, None])
        put(n + "1", np.concatenate([g[:64], np.ones(64, np.float32)])[:, None])
    cf[:, COL["eps"][0]] = EPS
    return cf


def matrices(i):
    z = np.zeros
    f = np.float32
    m = {}
    w = i["a_w_in"][0]
    m["ain"] = np.concatenate([w, z((D, 112), f)], 1)
    m["aout"] = i["a_w_out"][0]
    m["bq"] = i["b_w_q"][0]
    m["bout"] = i["b_w_out"][0]
    m["kv"] = i["w_kv"]
    for l in range(2):
        m[f"up{l}"], m[f"dn{l}"] = i["ffn_w_up"][l], i["ffn_w_down"][l]
        m[f"gu{l}"] = np.concatenate([i["ffn_w_gate_2"][l], i["ffn_w_up_2"][l]], 1)
        m[f"sd{l}"] = i["ffn_w_down_2"][l]
    e = i["even_w_in_2"][0]
    kp = e[:, 1664:1696]
    m["ei"] = np.concatenate([e[:, 1024:1408], e[:, 1408:1664], z((D, 64), f), kp, kp[:, 16:], kp[:, :16],
                              e[:, 0:512], e[:, 512:1024]], 1)
    uq = i["mla_w_uq_2"][0].reshape(384, 8, 96)
    m["uq"] = np.concatenate([uq, uq[:, :, 80:96], uq[:, :, 64:80]], 2).reshape(384, 1024)
    ukv = i["mla_w_ukv_2"][0].reshape(256, 8, 128)
    m["ukv"] = np.concatenate([np.concatenate([ukv[:, :, :64], z((256, 8, 64), f)], 2).reshape(256, 1024),
                               ukv[:, :, 64:].reshape(256, 512)], 1)
    m["eout"] = i["even_w_out_2"][0]
    m["oi"] = i["odd_w_in_2"][0]
    m["oout"] = i["odd_w_out_2"][0]
    return m


def host_w(i):
    plan = stream_plan()
    m = matrices(i)
    w = np.zeros((len(plan) // CT, 128, CT * 128), np.float32)
    for n, t in enumerate(plan):
        if t is not None:
            name, k, c = t
            o = n % CT * 128
            w[n // CT, :, o:o + 128] = m[name][128 * k:128 * k + 128, 128 * c:128 * c + 128]
    return w


def host_inputs(i):
    i = {k: np.asarray(v) for k, v in i.items()}
    o = host_consts()
    o["cf"] = host_cf(i)
    o["w"] = host_w(i)
    o["gmw"] = np.ascontiguousarray(i["gm_w_s_2"][0].transpose(2, 0, 1))
    o["gmb"] = np.ascontiguousarray(np.broadcast_to(i["gm_b_s_2"][0][None], (128, 4, 128)))
    o["xT"] = np.ascontiguousarray(i["x"][0].T.reshape(8, 128, S).transpose(1, 0, 2))
    return o


def kernel(**inputs):
    import concourse.bacc as bacc
    from concourse.bass_utils import run_bass_kernel_spmd

    arrays = host_inputs(inputs)
    nc = bacc.Bacc("TRN2", target_bir_lowering=False, num_devices=1)
    args = {n: nc.dram_tensor(f"in_{n}", v.shape, mybir.dt.from_np(v.dtype), kind="ExternalInput").ap()
            for n, v in arrays.items()}
    args["out"] = nc.dram_tensor("out_0", (128, 8, S), F32, kind="ExternalOutput").ap()
    build(nc, args)
    r = run_bass_kernel_spmd(nc, [{f"in_{n}": v for n, v in arrays.items()}], core_ids=[0])
    y = r.results[0]["out_0"]
    return np.ascontiguousarray(y.transpose(2, 1, 0).reshape(1, S, D))
```
